# Optimizing a Trainium2 kernel written in Bass

```python
import math
import jax, jax.numpy as jnp
from jax import lax
import numpy as np

D_MODEL = 1024
BATCH = 1
SEQ = 1024
DEPTH = 1

MEM_LEN = 256
N_MLSTM_HEADS = 4
MLSTM_HEAD_DIM = 128
MLSTM_WIDTH = N_MLSTM_HEADS * MLSTM_HEAD_DIM
CONV_WIDTH = 4
MLSTM_CHUNK = 128
N_DIFF_HEADS = 4
DIFF_QK_DIM = 64
DIFF_V_DIM = 2 * DIFF_QK_DIM
DIFF_WIDTH = N_DIFF_HEADS * DIFF_V_DIM
Q_BLOCK = 128
N_MEM_HEADS = 4
MEM_HEAD_DIM = 128
MEM_WIDTH = N_MEM_HEADS * MEM_HEAD_DIM
MIX_WIDTH = MLSTM_WIDTH + DIFF_WIDTH + MEM_WIDTH
IN_WIDTHS = (MLSTM_WIDTH, MLSTM_WIDTH, MLSTM_WIDTH,
             2 * N_DIFF_HEADS * DIFF_QK_DIM, 2 * N_DIFF_HEADS * DIFF_QK_DIM, DIFF_WIDTH, DIFF_WIDTH,
             MEM_WIDTH, MEM_WIDTH)
IN_WIDTH = 4608
NORM_EPS = 1e-6


def _split_cols(a, widths):
    offs = np.cumsum(widths)[:-1].tolist()
    return jnp.split(a, offs, axis=-1)

def rmsnorm(x, g):
    xf = x.astype(jnp.float32)
    y = xf * lax.rsqrt(jnp.mean(xf * xf, axis=-1, keepdims=True) + NORM_EPS)
    return (y * g.astype(jnp.float32)).astype(x.dtype)

def head_layernorm(h, g):
    mu = jnp.mean(h, axis=-1, keepdims=True)
    var = jnp.mean(jnp.square(h - mu), axis=-1, keepdims=True)
    y = (h - mu) * lax.rsqrt(var + NORM_EPS)
    y = y.reshape(h.shape[0], h.shape[1], -1)
    return y * g.astype(jnp.float32)

def causal_depthwise_conv(x, w, b):
    y = lax.conv_general_dilated(x, w[:, None, :], window_strides=(1,),
                                 padding=[(CONV_WIDTH - 1, 0)],
                                 dimension_numbers=('NWC', 'WIO', 'NWC'),
                                 feature_group_count=x.shape[-1])
    return y + b

def mlstm_chunkwise(q, k, v, i_pre, f_pre):
    B_, H_, S_, dh = q.shape
    L = MLSTM_CHUNK
    nc = S_ // L
    k = k * (dh ** -0.5)
    log_f = jax.nn.log_sigmoid(f_pre)

    def chunks(a):
        a = a.reshape((B_, H_, nc, L) + a.shape[3:])
        return jnp.moveaxis(a, 2, 0)

    qc, kc, vc, ic = chunks(q), chunks(k), chunks(v), chunks(i_pre)
    bc = jnp.cumsum(chunks(log_f), axis=-1)
    tri = jnp.tril(jnp.ones((L, L), dtype=bool))

    def step(carry, inp):
        C, n, m = carry
        qb, kb, vb, ib, bb = inp
        d = bb[..., :, None] - bb[..., None, :] + ib[..., None, :]
        d = jnp.where(tri, d, -jnp.inf)
        g = bb + m[..., None]
        m_t = jnp.maximum(g, jnp.max(d, axis=-1))
        s_qk = jnp.einsum('bhtk,bhsk->bhts', qb, kb) * jnp.exp(d - m_t[..., None])
        inter = jnp.exp(g - m_t)
        num = (jnp.einsum('bhts,bhsv->bhtv', s_qk, vb)
               + inter[..., None] * jnp.einsum('bhvk,bhtk->bhtv', C, qb))
        den = jnp.sum(s_qk, axis=-1) + inter * jnp.einsum('bhk,bhtk->bht', n, qb)
        h = num / jnp.maximum(jnp.abs(den), jnp.exp(-m_t))[..., None]
        b_end = bb[..., -1]
        a = b_end[..., None] - bb + ib
        m_new = jnp.maximum(b_end + m, jnp.max(a, axis=-1))
        wa = jnp.exp(a - m_new[..., None])
        decay = jnp.exp(b_end + m - m_new)
        C_new = decay[..., None, None] * C + jnp.einsum('bhs,bhsv,bhsk->bhvk', wa, vb, kb)
        n_new = decay[..., None] * n + jnp.einsum('bhs,bhsk->bhk', wa, kb)
        return (C_new, n_new, m_new), h

    init = (jnp.zeros((B_, H_, dh, dh), jnp.float32),
            jnp.zeros((B_, H_, dh), jnp.float32),
            jnp.zeros((B_, H_), jnp.float32))
    _, h = lax.scan(step, init, (qc, kc, vc, ic, bc))
    return jnp.moveaxis(h, 0, 2).reshape(B_, H_, S_, dh)

def diff_causal_attention(q, k, v, lam):
    S_ = q.shape[3]
    scale = DIFF_QK_DIM ** -0.5
    outs = []
    for j in range(S_ // Q_BLOCK):
        lo, hi = j * Q_BLOCK, (j + 1) * Q_BLOCK
        s = jnp.einsum('bhmqd,bhmkd->bhmqk', q[:, :, :, lo:hi], k[:, :, :, :hi]).astype(jnp.float32) * scale
        mask = jnp.arange(hi)[None, :] <= jnp.arange(lo, hi)[:, None]
        p = jax.nn.softmax(jnp.where(mask, s, -jnp.inf), axis=-1)
        pd = p[:, :, 0] - lam * p[:, :, 1]
        outs.append(jnp.einsum('bhqk,bhkd->bhqd', pd.astype(v.dtype), v[:, :, :hi]))
    return jnp.concatenate(outs, axis=2)

def first_inputs(seed: int = 0) -> dict:
    key = jax.random.key(seed)
    ks = jax.random.split(key, 24)
    nrm = jax.random.normal
    f32 = jnp.float32
    H = N_MLSTM_HEADS
    b_i = 0.1 * nrm(ks[10], (DEPTH, H), f32)
    b_f = 3.0 + 3.0 * jax.random.uniform(ks[11], (DEPTH, H), f32)
    return {
        'x': nrm(ks[0], (BATCH, SEQ, D_MODEL), f32),
        'mem': nrm(ks[1], (BATCH, MEM_LEN, D_MODEL), f32),
        'norm_g': 1.0 + 0.02 * nrm(ks[2], (DEPTH, D_MODEL), f32),
        'w_in': nrm(ks[3], (DEPTH, D_MODEL, IN_WIDTH), f32) * D_MODEL ** -0.5,
        'conv_w': nrm(ks[4], (DEPTH, CONV_WIDTH, MLSTM_WIDTH), f32) * CONV_WIDTH ** -0.5,
        'conv_b': 0.01 * nrm(ks[5], (DEPTH, MLSTM_WIDTH), f32),
        'wq_m': nrm(ks[6], (DEPTH, H, MLSTM_HEAD_DIM, MLSTM_HEAD_DIM), f32) * MLSTM_HEAD_DIM ** -0.5,
        'wk_m': nrm(ks[7], (DEPTH, H, MLSTM_HEAD_DIM, MLSTM_HEAD_DIM), f32) * MLSTM_HEAD_DIM ** -0.5,
        'wv_m': nrm(ks[8], (DEPTH, H, MLSTM_HEAD_DIM, MLSTM_HEAD_DIM), f32) * MLSTM_HEAD_DIM ** -0.5,
        'w_if': nrm(ks[9], (DEPTH, 3 * MLSTM_WIDTH, 2 * H), f32) * (3 * MLSTM_WIDTH) ** -0.5,
        'b_if': jnp.concatenate([b_i, b_f], axis=-1),
        'mnorm_g': 1.0 + 0.02 * nrm(ks[12], (DEPTH, MLSTM_WIDTH), f32),
        'skip_m': 1.0 + 0.02 * nrm(ks[13], (DEPTH, MLSTM_WIDTH), f32),
        'lam_q1': 0.1 * nrm(ks[14], (DEPTH, DIFF_QK_DIM), f32),
        'lam_k1': 0.1 * nrm(ks[15], (DEPTH, DIFF_QK_DIM), f32),
        'lam_q2': 0.1 * nrm(ks[16], (DEPTH, DIFF_QK_DIM), f32),
        'lam_k2': 0.1 * nrm(ks[17], (DEPTH, DIFF_QK_DIM), f32),
        'dnorm_g': 1.0 + 0.02 * nrm(ks[18], (DEPTH, DIFF_WIDTH), f32),
        'mem_norm_g': 1.0 + 0.02 * nrm(ks[19], (DEPTH, D_MODEL), f32),
        'w_mem_kv': nrm(ks[20], (DEPTH, D_MODEL, 2 * MEM_WIDTH), f32) * D_MODEL ** -0.5,
        'w_out': nrm(ks[21], (DEPTH, MIX_WIDTH, D_MODEL), f32) * MIX_WIDTH ** -0.5,
        'final_g': 1.0 + 0.02 * nrm(ks[22], (D_MODEL,), f32),
    }

def first_block(x, mem, norm_g, w_in, conv_w, conv_b, wq_m, wk_m, wv_m, w_if, b_if, mnorm_g, skip_m,
              lam_q1, lam_k1, lam_q2, lam_k2, dnorm_g, mem_norm_g, w_mem_kv, w_out, final_g):
    B_, S_, _ = x.shape
    Hm, dh = N_MLSTM_HEADS, MLSTM_HEAD_DIM
    Hd, Hc = N_DIFF_HEADS, N_MEM_HEADS
    for l in range(DEPTH):
        h = rmsnorm(x, norm_g[l])
        proj = h @ w_in[l]
        x_m, o_m, z_m, q_d, k_d, v_d, z_d, q_c, z_c = _split_cols(proj, IN_WIDTHS)

        x_cv = jax.nn.silu(causal_depthwise_conv(x_m, conv_w[l], conv_b[l]))
        xch = x_cv.reshape(B_, S_, Hm, dh)
        xmh = x_m.reshape(B_, S_, Hm, dh)
        q = jnp.einsum('bshd,hde->bshe', xch, wq_m[l])
        k = jnp.einsum('bshd,hde->bshe', xch, wk_m[l])
        v = jnp.einsum('bshd,hde->bshe', xmh, wv_m[l])
        qkv = jnp.concatenate([q, k, v], axis=2).reshape(B_, S_, 3 * MLSTM_WIDTH)
        gates = (qkv @ w_if[l] + b_if[l]).astype(jnp.float32)
        i_pre = jnp.transpose(gates[..., :Hm], (0, 2, 1))
        f_pre = jnp.transpose(gates[..., Hm:], (0, 2, 1))
        tr = lambda a: jnp.transpose(a.astype(jnp.float32), (0, 2, 1, 3))
        h_t = mlstm_chunkwise(tr(q), tr(k), tr(v), i_pre, f_pre)
        h_t = jnp.transpose(h_t, (0, 2, 1, 3))
        h_t = jax.nn.sigmoid(o_m.reshape(B_, S_, Hm, dh).astype(jnp.float32)) * h_t
        y_m = head_layernorm(h_t, mnorm_g[l]).astype(x.dtype)
        y_m = (y_m + skip_m[l] * x_cv) * jax.nn.silu(z_m)

        qd = jnp.transpose(q_d.reshape(B_, S_, Hd, 2, DIFF_QK_DIM), (0, 2, 3, 1, 4))
        kd = jnp.transpose(k_d.reshape(B_, S_, Hd, 2, DIFF_QK_DIM), (0, 2, 3, 1, 4))
        vd = jnp.transpose(v_d.reshape(B_, S_, Hd, DIFF_V_DIM), (0, 2, 1, 3))
        lam_init = 0.8 - 0.6 * math.exp(-0.3 * l)
        lam = (jnp.exp(jnp.sum(lam_q1[l].astype(jnp.float32) * lam_k1[l].astype(jnp.float32)))
               - jnp.exp(jnp.sum(lam_q2[l].astype(jnp.float32) * lam_k2[l].astype(jnp.float32)))
               + lam_init)
        od = jnp.transpose(diff_causal_attention(qd, kd, vd, lam), (0, 2, 1, 3))
        od = rmsnorm(od, dnorm_g[l].reshape(Hd, DIFF_V_DIM)) * (1.0 - lam_init)
        y_d = od.reshape(B_, S_, DIFF_WIDTH) * jax.nn.silu(z_d)

        kv = rmsnorm(mem, mem_norm_g[l]) @ w_mem_kv[l]
        km = kv[..., :MEM_WIDTH].reshape(B_, -1, Hc, MEM_HEAD_DIM)
        vm = kv[..., MEM_WIDTH:].reshape(B_, -1, Hc, MEM_HEAD_DIM)
        qc = q_c.reshape(B_, S_, Hc, MEM_HEAD_DIM)
        sc = jnp.einsum('bshd,bmhd->bhsm', qc, km).astype(jnp.float32) * MEM_HEAD_DIM ** -0.5
        pc = jax.nn.softmax(sc, axis=-1).astype(x.dtype)
        oc = jnp.einsum('bhsm,bmhd->bshd', pc, vm).reshape(B_, S_, MEM_WIDTH)
        y_c = oc * jax.nn.silu(z_c)

        y = jnp.concatenate([y_m, y_d, y_c], axis=-1) @ w_out[l]
        x = x + y
    return rmsnorm(x, final_g)


_first_inputs = first_inputs


def first_inputs(seed=0):
    import zlib

    import numpy as np

    out = dict(_first_inputs(seed))
    spreads = {}
    factors = {'norm_g': 3.08,
     'conv_b': 8.0,
     'mnorm_g': 200.0,
     'skip_m': 143.629,
     'lam_q1': 200.0,
     'dnorm_g': 200.0,
     'mem_norm_g': 59.701,
     'final_g': 22.327}
    for name, (base, spread) in spreads.items():
        noise = np.random.default_rng([zlib.crc32(name.encode()), seed]).standard_normal(out[name].shape)
        drawn = base * np.exp(spread * noise) if base else spread * noise
        out[name] = __import__('jax').numpy.asarray(drawn.astype(out[name].dtype))
    for name, factor in factors.items():
        out[name] = (out[name] * factor).astype(out[name].dtype)
    return out


_narrow_inputs = first_inputs


def first_inputs(seed=0):

    out = dict(_narrow_inputs(seed))
    wider = {'mnorm_g': 6.53, 'skip_m': 4.46, 'dnorm_g': 8.35, 'final_g': 3.16}
    for name, times in wider.items():
        mean = out[name].mean()
        out[name] = (mean + times * (out[name] - mean)).astype(out[name].dtype)
    return out


DEPTH_2 = 2

N_MIXERS = 2
SSM_GROUP = 16
SSM_GROUPS = D_MODEL // SSM_GROUP
SSM_STATE = 64
CONV_WIDTH_2 = 3
FFN_HIDDEN = ((8 * D_MODEL + 3 * 256 - 1) // (3 * 256)) * 256
N_SSM_LAYERS = (DEPTH_2 + 1) // 2
N_CONV_LAYERS = DEPTH_2 // 2
RMS_EPS = 1e-6
DT_MIN = 1e-3
DT_MAX = 1e-1


def rms_norm(x, g):
    x32 = x.astype(jnp.float32)
    y = x32 * lax.rsqrt(jnp.mean(x32 * x32, axis=-1, keepdims=True) + RMS_EPS)
    return (y * g.astype(jnp.float32)).astype(x.dtype)

def modulate(h, shift, scale):
    return h * (1.0 + scale) + shift

def _ssm_combine(e1, e2):
    a1r, a1i, b1r, b1i = e1
    a2r, a2i, b2r, b2i = e2
    ar = a2r * a1r - a2i * a1i
    ai = a2r * a1i + a2i * a1r
    br = a2r * b1r - a2i * b1i + b2r
    bi = a2r * b1i + a2i * b1r + b2i
    return (ar, ai, br, bi)

def s5_mixer(h, a_re, a_im, log_step, b_re, b_im, c_re, c_im, d, w_out):
    bsz, seqlen, _ = h.shape
    f32 = jnp.float32
    u = h.astype(f32).reshape(bsz, seqlen, SSM_GROUPS, SSM_GROUP)
    lr = jnp.minimum(a_re.astype(f32), -1e-4)
    li = a_im.astype(f32)
    dt = jnp.exp(log_step.astype(f32))[:, None]
    mag = jnp.exp(lr * dt)
    abr = mag * jnp.cos(li * dt)
    abi = mag * jnp.sin(li * dt)
    den = lr * lr + li * li
    qr = ((abr - 1.0) * lr + abi * li) / den
    qi = (abi * lr - (abr - 1.0) * li) / den
    br, bim = b_re.astype(f32), b_im.astype(f32)
    bbar_re = qr[..., None] * br - qi[..., None] * bim
    bbar_im = qr[..., None] * bim + qi[..., None] * br
    bu_re = jnp.einsum('blgh,gph->blgp', u, bbar_re)
    bu_im = jnp.einsum('blgh,gph->blgp', u, bbar_im)
    a_r = jnp.broadcast_to(abr[None, None], (1, seqlen, SSM_GROUPS, SSM_STATE))
    a_i = jnp.broadcast_to(abi[None, None], (1, seqlen, SSM_GROUPS, SSM_STATE))
    _, _, xr, xi = lax.associative_scan(_ssm_combine, (a_r, a_i, bu_re, bu_im), axis=1)
    y = (jnp.einsum('ghp,blgp->blgh', c_re.astype(f32), xr)
         - jnp.einsum('ghp,blgp->blgh', c_im.astype(f32), xi))
    y = y.reshape(bsz, seqlen, D_MODEL) + d.astype(f32) * h.astype(f32)
    y = jax.nn.gelu(y).astype(h.dtype)
    val, gate = jnp.split(y @ w_out, 2, axis=-1)
    return val * jax.nn.sigmoid(gate)

def short_conv_mixer(h, w_in, conv_w, w_out):
    bg, cg, v = jnp.split(h @ w_in, 3, axis=-1)
    cv = cg * v
    conv = lax.conv_general_dilated(
        cv, conv_w[:, None, :].astype(cv.dtype), window_strides=(1,),
        padding=[(CONV_WIDTH_2 - 1, 0)], dimension_numbers=('NWC', 'WIO', 'NWC'),
        feature_group_count=D_MODEL)
    return (bg * conv) @ w_out

def swiglu(h, w_in, w_out):
    g, u = jnp.split(h @ w_in, 2, axis=-1)
    return (jax.nn.silu(g) * u) @ w_out

def second_inputs(seed: int = 0) -> dict:
    key = jax.random.key(seed)
    ks = jax.random.split(key, 24)
    D, G, P, H, F = D_MODEL, SSM_GROUPS, SSM_STATE, SSM_GROUP, FFN_HIDDEN
    nrm = jax.random.normal
    x = nrm(ks[0], (BATCH, SEQ, D), jnp.float32)
    c = nrm(ks[1], (BATCH, D), jnp.float32)
    norm1_g = 1.0 + 0.02 * nrm(ks[2], (DEPTH_2, D), jnp.float32)
    norm2_g = 1.0 + 0.02 * nrm(ks[3], (DEPTH_2, D), jnp.float32)
    w_ada = 0.5 * D ** -0.5 * nrm(ks[4], (DEPTH_2, D, 6 * D), jnp.float32)
    b_ada = 0.01 * nrm(ks[5], (DEPTH_2, 6 * D), jnp.float32)
    n_idx = jnp.arange(P, dtype=jnp.float32)
    ssm_a_re = -0.5 + 0.01 * nrm(ks[6], (N_SSM_LAYERS, G, P), jnp.float32)
    ssm_a_im = math.pi * n_idx + 0.01 * nrm(ks[7], (N_SSM_LAYERS, G, P), jnp.float32)
    ssm_log_step = jax.random.uniform(ks[8], (N_SSM_LAYERS, G), jnp.float32,
                                      math.log(DT_MIN), math.log(DT_MAX))
    ssm_b_re = (2 * H) ** -0.5 * nrm(ks[9], (N_SSM_LAYERS, G, P, H), jnp.float32)
    ssm_b_im = (2 * H) ** -0.5 * nrm(ks[10], (N_SSM_LAYERS, G, P, H), jnp.float32)
    ssm_c_re = (2 * P) ** -0.5 * nrm(ks[11], (N_SSM_LAYERS, G, H, P), jnp.float32)
    ssm_c_im = (2 * P) ** -0.5 * nrm(ks[12], (N_SSM_LAYERS, G, H, P), jnp.float32)
    ssm_d = nrm(ks[13], (N_SSM_LAYERS, D), jnp.float32)
    ssm_w_out = D ** -0.5 * nrm(ks[14], (N_SSM_LAYERS, D, 2 * D), jnp.float32)
    conv_w_in = D ** -0.5 * nrm(ks[15], (N_CONV_LAYERS, D, 3 * D), jnp.float32)
    conv_w = CONV_WIDTH_2 ** -0.5 * nrm(ks[16], (N_CONV_LAYERS, CONV_WIDTH_2, D), jnp.float32)
    conv_w_out = D ** -0.5 * nrm(ks[17], (N_CONV_LAYERS, D, D), jnp.float32)
    w_ffn_in = D ** -0.5 * nrm(ks[18], (DEPTH_2, D, 2 * F), jnp.float32)
    w_ffn_out = F ** -0.5 * nrm(ks[19], (DEPTH_2, F, D), jnp.float32)
    final_g = 1.0 + 0.02 * nrm(ks[20], (D,), jnp.float32)
    return {"x": x, "c": c, "norm1_g": norm1_g, "norm2_g": norm2_g,
            "w_ada": w_ada, "b_ada": b_ada,
            "ssm_a_re": ssm_a_re, "ssm_a_im": ssm_a_im, "ssm_log_step": ssm_log_step,
            "ssm_b_re": ssm_b_re, "ssm_b_im": ssm_b_im,
            "ssm_c_re": ssm_c_re, "ssm_c_im": ssm_c_im,
            "ssm_d": ssm_d, "ssm_w_out": ssm_w_out,
            "conv_w_in": conv_w_in, "conv_w": conv_w, "conv_w_out": conv_w_out,
            "w_ffn_in": w_ffn_in, "w_ffn_out": w_ffn_out, "final_g": final_g}

def second_block(x, c, norm1_g, norm2_g, w_ada, b_ada,
              ssm_a_re, ssm_a_im, ssm_log_step, ssm_b_re, ssm_b_im,
              ssm_c_re, ssm_c_im, ssm_d, ssm_w_out,
              conv_w_in, conv_w, conv_w_out,
              w_ffn_in, w_ffn_out, final_g):
    c_act = jax.nn.silu(c)
    for i in range(DEPTH_2):
        mods = c_act @ w_ada[i] + b_ada[i]
        sh1, sc1, g1, sh2, sc2, g2 = [m[:, None, :] for m in jnp.split(mods, 6, axis=-1)]
        h = modulate(rms_norm(x, norm1_g[i]), sh1, sc1)
        j = i // N_MIXERS
        if i % N_MIXERS == 0:
            mix = s5_mixer(h, ssm_a_re[j], ssm_a_im[j], ssm_log_step[j],
                           ssm_b_re[j], ssm_b_im[j], ssm_c_re[j], ssm_c_im[j],
                           ssm_d[j], ssm_w_out[j])
        else:
            mix = short_conv_mixer(h, conv_w_in[j], conv_w[j], conv_w_out[j])
        x = x + g1 * mix
        h = modulate(rms_norm(x, norm2_g[i]), sh2, sc2)
        x = x + g2 * swiglu(h, w_ffn_in[i], w_ffn_out[i])
    return rms_norm(x, final_g)


def setup_inputs(seed=0):
    out = dict(first_inputs(seed))
    for name, value in second_inputs(seed + 1).items():
        if name != "x":
            out[name + "_2"] = value
    return out


def reference(
    x, mem, norm_g, w_in, conv_w, conv_b, wq_m, wk_m, wv_m, w_if, b_if, mnorm_g, skip_m, lam_q1,
    lam_k1, lam_q2, lam_k2, dnorm_g, mem_norm_g, w_mem_kv, w_out, final_g, c_2, norm1_g_2,
    norm2_g_2, w_ada_2, b_ada_2, ssm_a_re_2, ssm_a_im_2, ssm_log_step_2, ssm_b_re_2, ssm_b_im_2,
    ssm_c_re_2, ssm_c_im_2, ssm_d_2, ssm_w_out_2, conv_w_in_2, conv_w_2, conv_w_out_2,
    w_ffn_in_2, w_ffn_out_2, final_g_2,
):
    x = first_block(
        x, mem, norm_g, w_in, conv_w, conv_b, wq_m, wk_m, wv_m, w_if, b_if, mnorm_g, skip_m,
        lam_q1, lam_k1, lam_q2, lam_k2, dnorm_g, mem_norm_g, w_mem_kv, w_out, final_g,
    )
    return second_block(
        x, c_2, norm1_g_2, norm2_g_2, w_ada_2, b_ada_2, ssm_a_re_2, ssm_a_im_2, ssm_log_step_2,
        ssm_b_re_2, ssm_b_im_2, ssm_c_re_2, ssm_c_im_2, ssm_d_2, ssm_w_out_2, conv_w_in_2,
        conv_w_2, conv_w_out_2, w_ffn_in_2, w_ffn_out_2, final_g_2,
    )


_drawn_inputs = setup_inputs


def setup_inputs(seed=0):
    import zlib

    import numpy as np

    out = dict(_drawn_inputs(seed))
    spreads = {}
    factors = {'norm1_g_2': 8.0,
     'norm2_g_2': 8.0,
     'b_ada_2': 8.0,
     'ssm_a_re_2': 64.0,
     'ssm_a_im_2': 64.0,
     'ssm_log_step_2': 64.0,
     'ssm_b_re_2': 64.0,
     'ssm_b_im_2': 64.0,
     'ssm_c_re_2': 64.0,
     'ssm_c_im_2': 64.0,
     'ssm_d_2': 8.0,
     'ssm_w_out_2': 8.0,
     'conv_w_in_2': 3.141,
     'conv_w_2': 3.107,
     'conv_w_out_2': 3.113,
     'w_ffn_in_2': 4.044,
     'w_ffn_out_2': 4.039,
     'final_g_2': 7.932}
    for name, (base, spread) in spreads.items():
        noise = np.random.default_rng([zlib.crc32(name.encode()), seed]).standard_normal(out[name].shape)
        drawn = base * np.exp(spread * noise) if base else spread * noise
        out[name] = __import__('jax').numpy.asarray(drawn.astype(out[name].dtype))
    for name, factor in factors.items():
        out[name] = (out[name] * factor).astype(out[name].dtype)
    return out
```

```python
from contextlib import ExitStack

import concourse.bass as bass
from concourse import mybir

ALU = mybir.AluOpType
ACT = mybir.ActivationFunctionType
AX = mybir.AxisListType
F32 = mybir.dt.float32
F32R = mybir.dt.float32r

P = 128
D = 1024
S = 1024
KD = D // P
TQ = S // P
MEM = 256
HEADS = 4
F = 2816
FT = F // P
FFN_PARTS = (8, 8, 6)
EPS = 1e-6
BANK = 512
NEG = -1.0e30
TWO_PI = 6.283185307179586
GROUPS, SSM_STATE, GROUP_W = 64, 64, 16
STEP = 8
NSTEP = S // STEP
QPAIRS = 8
PASSES = GROUPS // 2 // QPAIRS

COLS = {}
_at = 0
for _name, _n in (("norm_g", 8), ("mem_norm_g", 8), ("final_g", 8), ("conv", 20), ("mnorm_skip", 8),
                  ("dnorm_g", 4), ("norm1_g_2", 16), ("norm2_g_2", 16), ("b_ada_2", 96), ("ssm_d_2", 8),
                  ("conv_w_2", 24), ("final_g_2", 8), ("c_2", 8)):
    COLS[_name] = (_at, _n)
    _at += _n
NCOLS = _at


class Steps:

    def __init__(self, sem, names):
        self.sem, self.names = sem, names
        self.done = {n: i + 1 for i, n in enumerate(names)}

    def after(self, name, turn=0):
        return self.sem, turn * len(self.names) + self.done[name]


def flat(ap):
    return ap.rearrange("p a s -> p (a s)")


def at(t, i):
    return flat(t[:, bass.ds(i, 1), :])


def build(nc, a, out, upto="end"):
    with ExitStack() as whole:
        def sem(name):
            return whole.enter_context(nc.semaphore(name))

        def dram(name, shape):
            return nc.dram_tensor(name, shape, F32).ap()

        xT = whole.enter_context(nc.sbuf_tensor("xT", [P, KD, S], F32))
        stage = whole.enter_context(nc.sbuf_tensor("stage", [P, 2, KD * P], F32))
        wH = whole.enter_context(nc.sbuf_tensor("wH", [P, 2, KD * P], F32R))
        wL = whole.enter_context(nc.sbuf_tensor("wL", [P, 2, KD * P], F32R))
        ident = whole.enter_context(nc.sbuf_tensor("ident", [P, P], F32))
        ones = whole.enter_context(nc.sbuf_tensor("ones", [P, P], F32))
        col = whole.enter_context(nc.sbuf_tensor("col", [P, NCOLS], F32))
        mods = whole.enter_context(nc.sbuf_tensor("mods", [P, 96], F32))
        gain = whole.enter_context(nc.sbuf_tensor("gain", [P, 4 * KD], F32))
        eps = whole.enter_context(nc.sbuf_tensor("eps", [P, 1], F32))
        accA = [whole.enter_context(nc.psum_tensor(f"accA{i}", [P, S], F32)) for i in range(2)]
        accB = [whole.enter_context(nc.psum_tensor(f"accB{i}", [P, S], F32)) for i in range(2)]

        def c_(name, i):
            return col[:, COLS[name][0] + i:COLS[name][0] + i + 1]

        stage_free = sem("stage_free")
        staged = [sem("staged0"), sem("staged1")]
        w_hi = sem("w_hi")
        w_lo = sem("w_lo")
        tile_done = sem("tile_done")
        psum_free = [sem("psum_free0"), sem("psum_free1")]
        stream = {"tile": 0}

        def weight_stream(segs, block, before=None, beside=None):
            for s in segs:
                s["t0"] = stream["tile"]
                s["body"] = len(s["act"])
                stream["tile"] += s["iters"] * s["body"]

            def tile_of(s, i, p):
                return i * s["body"] + (s["t0"] + p)

            @block.sync
            def _(sp):
                for s in segs:
                    n = s["K"] * P

                    def load(i, p):
                        sp.wait_ge(stage_free, tile_of(s, i, p) + 1)
                        sp.dma_start(stage[:, p % 2, 0:n], s["w"][i * s["body"] + p]).then_inc(staged[p % 2], 16)
                        if beside is not None:
                            beside["sp"](sp, i * s["body"] + p)
                    with sp.Fori(0, s["iters"]) as i:
                        for p in range(s["body"]):
                            load(i, p)

            def act_split(act, s, i, p):
                n = s["K"] * P
                b = p % 2
                act.wait_ge(staged[b], i * (8 * s["body"]) + 16 * ((s["t0"] + p) // 2 + 1))
                act.wait_ge(tile_done, tile_of(s, i, p) + 1)
                act.activation(wH[:, b, 0:n], stage[:, b, 0:n], ACT.Copy).then_inc(w_hi, 1)

            def dve_split(dve, s, i, p):
                n = s["K"] * P
                b = p % 2
                dve.wait_ge(w_hi, tile_of(s, i, p) + 1)
                dve.tensor_tensor(wL[:, b, 0:n], stage[:, b, 0:n], wH[:, b, 0:n].bitcast(F32),
                                  ALU.subtract).then_inc(w_lo, 1)

            def dve_split_inc(dve, s, i, p):
                dve_split(dve, s, i, p)
                dve.wait_ge(w_lo, tile_of(s, i, p) + 1)
                dve.sem_inc(stage_free, 1)

            def walk(eng, split, key):
                split(eng, segs[0], 0, 0)
                if before is not None:
                    split(eng, segs[0], 0, 1)
                    before[key](eng)
                for j, s in enumerate(segs):
                    def step(i, last, split_already=False):
                        for p in range(s["body"]):
                            if p + 1 < s["body"]:
                                if not (split_already and p == 0):
                                    split(eng, s, i, p + 1)
                            elif not last:
                                split(eng, s, i + 1, 0)
                            elif j + 1 < len(segs):
                                split(eng, segs[j + 1], 0, 0)
                            if s[key][p] is not None:
                                s[key][p](eng, i, tile_of(s, i, p) + 3, accA[p % 2], psum_free[p % 2])
                    start = 0
                    if j == 0 and before is not None:
                        step(0, False, True)
                        start = 1
                    if s["iters"] - 1 > start:
                        with eng.Fori(start, s["iters"] - 1) as i:
                            step(i, False)
                    step(s["iters"] - 1, True)
                if beside is not None and key == "dve":
                    beside["dve"](eng)

            @block.scalar
            def _(act):
                walk(act, act_split, "act")

            @block.vector
            def _(dve):
                walk(dve, dve_split_inc, "dve")

            @block.tensor
            def _(pe):
                if before is not None:
                    before["pe"](pe)
                for j, s in enumerate(segs):
                    def tile(i, p, first=False):
                        cols = s["cols"]
                        b = p % 2
                        if p == 0 and s["ready"] is not None:
                            pe.wait_ge(*s["ready"])
                        pe.wait_ge(w_lo, tile_of(s, i, p) + 1)
                        pe.wait_ge(psum_free[b], i * (s["body"] // 2) + ((s["t0"] + p) // 2 + 1))
                        for k in range(s["K"]):
                            if first:
                                pe.wait_ge(*before["ready"](k))
                            for wpart, xpart in ((wH, 0), (wH, 1), (wL, 0)):
                                for c0 in range(0, cols, BANK):
                                    c1 = min(cols, c0 + BANK)
                                    last = pe.matmul(accA[b][:, c0:c1], wpart[:, b, k * P:(k + 1) * P],
                                                     s["rhs"](xpart, k)[:, c0:c1],
                                                     start=(k == 0 and wpart is wH and xpart == 0),
                                                     stop=(k == s["K"] - 1 and wpart is wL))
                        last.then_inc(tile_done, 1)
                        if beside is not None:
                            beside["pe"](pe, i * s["body"] + p)
                    start = 0
                    if j == 0 and before is not None:
                        for p in range(s["body"]):
                            tile(0, p, first=(p == 0))
                        start = 1
                    with pe.Fori(start, s["iters"]) as i:
                        for p in range(s["body"]):
                            tile(i, p)

        ld = sem("params_loaded")
        set_ = sem("constants_set")
        with nc.Block() as block:
            @block.sync
            def _(sp):
                sp.dma_start(xT[:, :, :], a["xT"].rearrange("(k p) s -> p k s", p=P)).then_inc(ld, 16)
                sp.dma_start(col[:, :], a["cols"]).then_inc(ld, 16)
                sp.dma_start(ident[:, :], a["ident"]).then_inc(ld, 16)
                sp.sem_inc(stage_free, 2)
                sp.sem_inc(tile_done, 2)
                sp.sem_inc(psum_free[0], 1)
                sp.sem_inc(psum_free[1], 1)
                sp.wait_ge(ld, 48)

            @block.vector
            def _(dve):
                dve.memset(ones[:, :], 1.0).then_inc(set_, 1)
                dve.memset(eps[:, :], EPS).then_inc(set_, 1)

        nsq = sem("norm_squared")
        nadd = sem("norm_added")
        nsum = sem("norm_summed")
        nroot = sem("norm_root")
        nrec = sem("norm_reciprocal")
        nmul = sem("norm_scaled")
        nhi = sem("norm_hi")
        nlo = sem("norm_lo")
        ncount = {"n": 0}

        def norm(src, n, gain_col, shift_col, **where):
            r = ncount["n"]
            with ExitStack() as es:
                bufs = [es.enter_context(nc.sbuf_tensor(f"norm{r}_{m}", [P, n], F32)) for m in range(3)]
                progs = norm_programs(bufs, src, n, gain_col, shift_col, **where)
                block = es.enter_context(nc.Block())
                block.scalar(progs["act"])
                block.vector(progs["dve"])
                block.tensor(progs["pe"])

        def norm_programs(bufs, src, n, gain_col, shift_col, hi=None, lo=None, full=None, steps=False):
            r = ncount["n"]
            ncount["n"] += 1
            sq = xn = bufs[0:2]
            tot = rstd = bufs[2]
            b8, b1 = r * KD, r

            def act_program(act):
                for k in range(KD):
                    if k >= 2:
                        act.wait_ge(nadd, b8 + k - 1)
                    act.activation(sq[k % 2][:, :], src(k), ACT.Square).then_inc(nsq, 1)
                act.wait_ge(nsum, b1 + 1)
                act.activation(rstd[:, :], accB[1][:, 0:n], ACT.Sqrt, scale=1.0 / D,
                               bias=eps[:, 0:1]).then_inc(nroot, 1)
                for k in range(KD):
                    act.wait_ge(nmul, b8 + k + 1)
                    dst = hi(k) if hi is not None else full(k)
                    x_k = xn[k % 2][:, :]
                    if steps:
                        x_k = x_k.rearrange("p (c j) -> p c j", j=STEP)
                    if shift_col is None:
                        act.activation(dst, x_k, ACT.Copy).then_inc(nhi, 1)
                    else:
                        act.activation(dst, x_k, ACT.Identity,
                                       bias=shift_col(k)).then_inc(nhi, 1)

            def dve_program(dve):
                for k in range(KD):
                    dve.wait_ge(nsq, b8 + k + 1)
                    if k == 0:
                        dve.tensor_copy(tot[:, :], sq[0][:, :]).then_inc(nadd, 1)
                    else:
                        dve.wait_ge(nadd, b8 + k)
                        dve.tensor_tensor(tot[:, :], tot[:, :], sq[k % 2][:, :], ALU.add).then_inc(nadd, 1)
                dve.wait_ge(nroot, b1 + 1)
                dve.reciprocal(rstd[:, :], rstd[:, :]).then_inc(nrec, 1)
                dve.wait_ge(nrec, b1 + 1)

                def scaled(k):
                    if k >= 2:
                        dve.wait_ge(nhi, b8 + k - 1)
                        if hi is not None:
                            dve.wait_ge(nlo, b8 + k - 1)
                    dve.scalar_tensor_tensor(out=xn[k % 2][:, :], in0=src(k), scalar=gain_col(k),
                                             in1=rstd[:, :], op0=ALU.mult, op1=ALU.mult).then_inc(nmul, 1)

                def low(k):
                    if hi is None:
                        return
                    dve.wait_ge(nhi, b8 + k + 1)
                    dve.wait_ge(nmul, b8 + k + 1)
                    h32 = hi(k).bitcast(F32)
                    if shift_col is None:
                        dve.tensor_tensor(lo(k), xn[k % 2][:, :], h32, ALU.subtract).then_inc(nlo, 1)
                    else:
                        dve.scalar_tensor_tensor(out=lo(k), in0=xn[k % 2][:, :], scalar=shift_col(k),
                                                 in1=h32, op0=ALU.add, op1=ALU.subtract).then_inc(nlo, 1)
                scaled(0)
                for k in range(1, KD):
                    scaled(k)
                    low(k - 1)
                low(KD - 1)
                if hi is None:
                    dve.sem_inc(nlo, KD)

            def pe_program(pe):
                pe.wait_ge(nadd, b8 + KD)
                for c0 in range(0, n, BANK):
                    c1 = min(n, c0 + BANK)
                    last = pe.matmul(accB[1][:, c0:c1], ones[:, :], tot[:, c0:c1], start=True, stop=True)
                last.then_inc(nsum, 1)
            return dict(act=act_program, dve=dve_program, pe=pe_program, ready=lambda k: (nlo, b8 + k + 1))

        stored = sem("stored")
        stores = {"n": 0}

        def stage_end(name):
            return upto == name

        def store_out(src, order=None):
            with nc.Block() as block:
                @block.sync
                def _(sp):
                    sp.dma_start(out.rearrange("(k p) s -> p k s", p=P), src).then_inc(stored, 16)
                    sp.wait_ge(stored, 16)

        def copy_to(dst, step, p):
            def epi(act, i, done, acc, psum_free):
                act.wait_ge(tile_done, done)
                act.activation(at(dst, i * step + p), acc[:, :], ACT.Copy).then_inc(psum_free, 1)
            return epi

        def add_to_x(p, gate=None):
            def epi(dve, i, done, acc, psum_free):
                dve.wait_ge(tile_done, done)
                x_m = at(xT, i * 2 + p)
                if gate is None:
                    dve.tensor_tensor(x_m, acc[:, :], x_m, ALU.add).then_inc(psum_free, 1)
                else:
                    dve.scalar_tensor_tensor(out=x_m, in0=acc[:, :], scalar=mods[:, bass.ds(i * 2 + (gate + p), 1)],
                                             in1=x_m, op0=ALU.mult, op1=ALU.add).then_inc(psum_free, 1)
            return epi

        ADA_PER = 4
        cact_set = sem("c_activated")
        ada_in = [sem(f"ada_landed{b}") for b in range(ADA_PER)]
        ada_mul = sem("ada_multiplied")
        ada_add = sem("ada_added")
        cact = whole.enter_context(nc.sbuf_tensor("cact", [P, KD], F32))
        with nc.Block() as block:
            @block.scalar
            def _(act):
                act.activation(cact[:, :], col[:, COLS["c_2"][0]:COLS["c_2"][0] + KD], ACT.Silu).then_inc(cact_set, 1)

            @block.tensor
            def _(pe):
                pe.sem_inc(ada_mul, ADA_PER)

        def modulation(wada, n0, ntiles):
            def on_sp(sp, n):
                for b in range(ADA_PER):
                    sp.wait_ge(ada_mul, n * ADA_PER + (n0 * ADA_PER + b + 1))
                    sp.dma_start(wada[:, b, :], a["w_ada_2"][n * ADA_PER + (n0 * ADA_PER + b)]).then_inc(ada_in[b], 16)

            def on_pe(pe, n):
                for b in range(ADA_PER):
                    pe.wait_ge(ada_in[b], n * 16 + (n0 * 16 + 16))
                    for k in range(KD):
                        last = pe.matmul(accB[0][:, bass.ds(n * ADA_PER + (n0 * ADA_PER + b), 1)],
                                         wada[:, b, k * P:(k + 1) * P], cact[:, k:k + 1],
                                         start=(k == 0), stop=(k == KD - 1))
                    last.then_inc(ada_mul, 1)

            def on_dve(dve):
                c0, c1 = n0 * ADA_PER, (n0 + ntiles) * ADA_PER
                b0 = COLS["b_ada_2"][0]
                dve.wait_ge(ada_mul, ADA_PER + c1)
                dve.tensor_tensor(mods[:, c0:c1], accB[0][:, c0:c1], col[:, b0 + c0:b0 + c1], ALU.add).then_inc(ada_add, 1)
            return dict(sp=on_sp, pe=on_pe, dve=on_dve)

        def modulation_gains():
            with nc.Block() as block:
                @block.vector
                def _(dve):
                    for n, (name, layer, part) in enumerate((("norm1_g_2", 0, 1), ("norm2_g_2", 0, 4),
                                                             ("norm1_g_2", 1, 1), ("norm2_g_2", 1, 4))):
                        sc = layer * 48 + part * KD
                        g0 = COLS[name][0] + layer * KD
                        dve.scalar_tensor_tensor(out=gain[:, n * KD:(n + 1) * KD], in0=mods[:, sc:sc + KD], scalar=1.0,
                                                 in1=col[:, g0:g0 + KD], op0=ALU.add, op1=ALU.mult).then_inc(ada_add, 1)
        with ExitStack() as first:
            hH = first.enter_context(nc.sbuf_tensor("hH", [P, KD, S], F32R))
            hL = first.enter_context(nc.sbuf_tensor("hL", [P, KD, S], F32R))

            def h_of(part, k):
                return (hH, hL)[part][:, k, :]

            projected = {"n": 0}

            def project(dst, tile0, ntiles):
                n0 = projected["n"]
                projected["n"] += ntiles
                with ExitStack() as es:
                    wada = es.enter_context(nc.sbuf_tensor(f"wada{n0}", [P, ADA_PER, KD * P], F32))
                    before = None
                    if n0 == 0:
                        bufs = [es.enter_context(nc.sbuf_tensor(f"norm_first{m}", [P, S], F32)) for m in range(3)]
                        before = norm_programs(bufs, lambda k: xT[:, k, :], S, lambda k: c_("norm_g", k), None,
                                               hi=lambda k: hH[:, k, :], lo=lambda k: hL[:, k, :])
                    block = es.enter_context(nc.Block())
                    weight_stream([dict(w=a["w_in"][tile0:tile0 + ntiles], K=KD, iters=ntiles // 2,
                                        act=[copy_to(dst, 2, 0), copy_to(dst, 2, 1)], dve=[None, None],
                                        rhs=h_of, cols=S, ready=None)], block, before, modulation(wada, n0, ntiles))

            z_silu = sem("z_silu")
            z_mul = sem("z_gated")
            z_hi = sem("z_hi")
            z_lo = sem("z_lo")
            mixers = {"n": 0}

            def gate_and_project(y, y0, sz, ztile0, part):
                base = mixers["n"] * HEADS
                mixers["n"] += 1
                with ExitStack() as es:
                    mixH = es.enter_context(nc.sbuf_tensor(f"mixH{part}", [P, HEADS, S], F32R))
                    mixL = es.enter_context(nc.sbuf_tensor(f"mixL{part}", [P, HEADS, S], F32R))
                    block = es.enter_context(nc.Block())

                    def act_z(p):
                        def epi(act, i, done, acc, psum_free):
                            act.wait_ge(tile_done, done)
                            if p == 1:
                                act.wait_ge(z_mul, i * 2 + (base + 1))
                            act.activation(sz, acc[:, :], ACT.Silu).then_inc(z_silu, 1)
                            act.wait_ge(z_mul, i * 2 + (base + p + 1))
                            act.activation(at(mixH, i * 2 + p), at(y, i * 2 + (y0 + p)), ACT.Copy).then_inc(z_hi, 1)
                        return epi

                    def dve_z(p):
                        def epi(dve, i, done, acc, psum_free):
                            y_m = at(y, i * 2 + (y0 + p))
                            dve.wait_ge(z_silu, i * 2 + (base + p + 1))
                            dve.tensor_tensor(y_m, y_m, sz, ALU.mult).then_inc(z_mul, 1)
                            dve.wait_ge(z_hi, i * 2 + (base + p + 1))
                            dve.tensor_tensor(at(mixL, i * 2 + p), y_m, at(mixH, i * 2 + p).bitcast(F32),
                                              ALU.subtract).then_inc(z_lo, 1)
                            dve.wait_ge(z_lo, i * 2 + (base + p + 1))
                            dve.sem_inc(psum_free, 1)
                        return epi
                    weight_stream([
                        dict(w=a["w_in"][ztile0:ztile0 + HEADS], K=KD, iters=HEADS // 2, act=[act_z(0), act_z(1)],
                             dve=[dve_z(0), dve_z(1)], rhs=h_of, cols=S, ready=None),
                        dict(w=a["w_out"][part], K=HEADS, iters=KD // 2, act=[None, None],
                             dve=[add_to_x(0), add_to_x(1)], rhs=lambda q, k: (mixH, mixL)[q][:, k, :],
                             cols=S, ready=(z_lo, base + HEADS))], block)

            mlstm_mixer(nc, a, locals())
            if stage_end("M"):
                store_out(xT[:, :, :])
                return
            diff_mixer(nc, a, locals())
            if stage_end("D"):
                store_out(xT[:, :, :])
                return
            memory_mixer(nc, a, locals())
            if stage_end("C"):
                store_out(xT[:, :, :])
                return
        norm(lambda k: xT[:, k, :], S, lambda k: c_("final_g", k), None, full=lambda k: xT[:, k, :])
        if stage_end("first"):
            store_out(xT[:, :, :])
            return
        modulation_gains()
        second_block(nc, a, locals())
        if upto[:3] in ("mix", "ffn"):
            store_out(xT[:, :, :])
            return
        norm(lambda k: xT[:, k, :], S, lambda k: c_("final_g_2", k), None, full=lambda k: xT[:, k, :])
        store_out(xT[:, :, :])


def mlstm_mixer(nc, a, env):
    sem, col, ident, ones, eps, stage = (env[k] for k in ("sem", "col", "ident", "ones", "eps", "stage"))
    accA, accB = env["accA"], env["accB"]
    SCALE = float(P) ** -0.5
    with ExitStack() as mix:
        pm = mix.enter_context(nc.sbuf_tensor("pm", [P, 2 * HEADS, S], F32))
        env["project"](pm, 0, 2 * HEADS)
        with ExitStack() as es:
            def sb(name, shape, where=es):
                return where.enter_context(nc.sbuf_tensor(name, shape, F32))
            xcv = sb("xcv", [P, HEADS, S])
            acol = sb("acol", [P, TQ, HEADS])
            wcol = sb("wcol", [P, TQ, HEADS])
            rows_d = nc.dram_tensor("gate_rows", [HEADS, 3, S], F32).ap()

            with ExitStack() as g:
                gi = sb("gi", [HEADS, S], g)
                gf = sb("gf", [HEADS, S], g)
                g1 = ExitStack()
                cw = sb("cw", [P, 5], g1)
                xc = sb("xc", [P, S], g1)
                wh = sb("gate_w_head", [P, 3 * P], g1)
                wg = sb("gate_w_if", [P, 3 * 8], g1)
                qkv = sb("gate_qkv", [P, 3, S], g1)
                in_w = sem("gates_w_landed")
                A = Steps(sem("gates_act"), ["conv", "q", "v"])
                V = Steps(sem("gates_dve"), ["cols", "tap3", "tap2", "tap1", "tap0", "k", "gi", "gf"])
                T = Steps(sem("gates_pe"), ["q", "k", "v", "gi", "gf"])
                free = sem("gates_head_free")
                setg = sem("gates_zeroed")
                with nc.Block() as block:
                    @block.sync
                    def _(sp):
                        with sp.Fori(0, HEADS) as h:
                            sp.wait_ge(free, h + 1)
                            sp.dma_start(wh[:, :], a["w_qkv"][h]).then_inc(in_w, 16)
                            sp.dma_start(wg[:, :], a["w_if"][h]).then_inc(in_w, 16)

                    @block.vector
                    def _(dve):
                        dve.memset(gi[:, :], 0.0).then_inc(setg, 1)
                        dve.memset(gf[:, :], 0.0).then_inc(setg, 1)
                        dve.wait_ge(setg, 2)
                        dve.sem_inc(free, 1)
                        c0 = COLS["conv"][0]
                        with dve.Fori(0, HEADS) as h:
                            dve.tensor_copy(cw[:, :], col[:, bass.ds(h * 5 + c0, 5)]).then_inc(V.sem, 1)
                            x_m = pm[:, bass.ds(h, 1), :]
                            dve.wait_ge(*V.after("cols", h))
                            dve.tensor_scalar(xc[:, :], flat(x_m), cw[:, 3:4], cw[:, 4:5], ALU.mult,
                                              ALU.add).then_inc(V.sem, 1)
                            for n, back in (("tap3", 1), ("tap2", 2), ("tap1", 3)):
                                dve.wait_ge(*V.after(n, h))
                                dve.scalar_tensor_tensor(
                                    out=xc[:, back:S], in0=flat(x_m[:, :, 0:S - back]), scalar=cw[:, 3 - back:4 - back],
                                    in1=xc[:, back:S], op0=ALU.mult, op1=ALU.add).then_inc(V.sem, 1)
                            dve.wait_ge(*T.after("k", h))
                            dve.tensor_copy(qkv[:, 1, :], accA[1][:, :]).then_inc(V.sem, 1)
                            dve.wait_ge(*T.after("gi", h))
                            dve.tensor_tensor(gi[:, :], accB[1][0:HEADS, :], gi[:, :], ALU.add).then_inc(V.sem, 1)
                            dve.wait_ge(*T.after("gf", h))
                            dve.tensor_tensor(gf[:, :], accA[0][0:HEADS, :], gf[:, :], ALU.add).then_inc(V.sem, 1)
                            dve.wait_ge(*V.after("gf", h))
                            dve.sem_inc(free, 1)

                    @block.scalar
                    def _(act):
                        with act.Fori(0, HEADS) as h:
                            act.wait_ge(*V.after("tap0", h))
                            act.activation(at(xcv, h), xc[:, :], ACT.Silu).then_inc(A.sem, 1)
                            act.wait_ge(*T.after("q", h))
                            act.activation(qkv[:, 0, :], accA[0][:, :], ACT.Copy).then_inc(A.sem, 1)
                            act.wait_ge(*T.after("v", h))
                            act.activation(qkv[:, 2, :], accB[0][:, :], ACT.Copy).then_inc(A.sem, 1)

                    @block.tensor
                    def _(pe):
                        with pe.Fori(0, HEADS) as h:
                            pe.wait_ge(in_w, h * 32 + 32)
                            pe.wait_ge(*A.after("conv", h))
                            for n, (acc, src) in enumerate(((accA[0], xcv), (accA[1], xcv), (accB[0], pm))):
                                for c0 in (0, BANK):
                                    last = pe.matmul(acc[:, c0:c0 + BANK], wh[:, n * P:(n + 1) * P],
                                                     flat(src[:, bass.ds(h, 1), c0:c0 + BANK]), start=True, stop=True)
                                last.then_inc(T.sem, 1)
                            pe.wait_ge(*A.after("v", h))
                            pe.wait_ge(*V.after("k", h))
                            for acc, w0 in ((accB[1], 0), (accA[0], HEADS)):
                                for c0 in (0, BANK):
                                    for n in range(3):
                                        last = pe.matmul(acc[0:HEADS, c0:c0 + BANK], wg[:, n * 8 + w0:n * 8 + w0 + HEADS],
                                                         qkv[:, n, c0:c0 + BANK], start=(n == 0), stop=(n == 2))
                                last.then_inc(T.sem, 1)

                g1.close()
                t1 = sb("gate_t", [HEADS, S], g)
                rows = sb("gate_rows_sb", [HEADS, 3, S], g)
                bif = sb("gate_bias", [HEADS, 2], g)
                keep = sb("gate_keep", [HEADS, S], g)
                mlast = sb("gate_m", [HEADS, TQ + 1], g)
                in_g = sem("gate_consts_landed")
                rows_out = sem("gate_rows_stored")
                A = Steps(sem("rows_act"), ["abs", "exp", "ln"] + [f"inter{c}" for c in range(TQ)]
                          + [f"wa{c}" for c in range(TQ)] + ["en"])
                V = Steps(sem("rows_dve"), ["gi", "gf", "keep", "m0", "logf", "b", "a"]
                          + [x for c in range(TQ) for x in (f"M{c}", f"m{c + 1}")] + ["negM", "mt", "acol", "wcol"])
                T = Steps(sem("rows_pe"), ["a", "wa"])
                with nc.Block() as block:
                    @block.sync
                    def _(sp):
                        sp.dma_start(bif[:, :], a["b_if"]).then_inc(in_g, 16)
                        sp.wait_ge(*A.after("en"))
                        sp.wait_ge(*V.after("negM"))
                        sp.dma_start(rows_d, rows[:, :, :]).then_inc(rows_out, 16)
                        sp.wait_ge(rows_out, 16)

                    @block.vector
                    def _(dve):
                        dve.wait_ge(in_g, 16)
                        dve.tensor_scalar(gi[:, :], gi[:, :], bif[:, 0:1], None, ALU.add).then_inc(V.sem, 1)
                        dve.tensor_scalar(gf[:, :], gf[:, :], bif[:, 1:2], None, ALU.add).then_inc(V.sem, 1)
                        dve.memset(keep[:, :], 1.0).then_inc(V.sem, 1)
                        dve.wait_ge(*V.after("keep"))
                        dve.memset(keep[:, :].rearrange("p (c t) -> p c t", t=P)[:, :, 0:1], 0.0)
                        dve.memset(mlast[:, 0:1], 0.0).then_inc(V.sem, 1)
                        dve.wait_ge(*A.after("ln"))
                        dve.scalar_tensor_tensor(out=gf[:, :], in0=gf[:, :], scalar=0.0, in1=t1[:, :],
                                                 op0=ALU.min, op1=ALU.subtract).then_inc(V.sem, 1)
                        dve.wait_ge(*V.after("logf"))
                        dve.tensor_tensor_scan(t1[:, :], keep[:, :], gf[:, :], 0.0, ALU.mult, ALU.add).then_inc(V.sem, 1)
                        dve.wait_ge(*V.after("b"))
                        dve.tensor_tensor(gi[:, :], gi[:, :], t1[:, :], ALU.subtract).then_inc(V.sem, 1)
                        dve.wait_ge(*V.after("a"))
                        for c in range(TQ):
                            k = slice(c * P, (c + 1) * P)
                            end = (c + 1) * P - 1
                            if c:
                                dve.wait_ge(*V.after(f"m{c}"))
                            dve.tensor_tensor_scan(gf[:, k], gi[:, k], gi[:, k], mlast[:, c:c + 1],
                                                   ALU.max, ALU.max).then_inc(V.sem, 1)
                            dve.wait_ge(*V.after(f"M{c}"))
                            dve.tensor_tensor(mlast[:, c + 1:c + 2], t1[:, end:end + 1], gf[:, end:end + 1],
                                              ALU.add).then_inc(V.sem, 1)
                        dve.tensor_scalar(rows[:, 0, :], gf[:, :], -1.0, None, ALU.mult).then_inc(V.sem, 1)
                        dve.tensor_tensor(rows[:, 2, :], gf[:, :], t1[:, :], ALU.add).then_inc(V.sem, 1)
                        dve.wait_ge(*T.after("a"))
                        dve.tensor_copy(acol[:, :, :], accA[0][:, 0:TQ * HEADS].rearrange("p (c h) -> p c h", h=HEADS)
                                        ).then_inc(V.sem, 1)
                        dve.wait_ge(*T.after("wa"))
                        dve.tensor_copy(wcol[:, :, :], accA[1][:, 0:TQ * HEADS].rearrange("p (c h) -> p c h", h=HEADS)
                                        ).then_inc(V.sem, 1)

                    @block.scalar
                    def _(act):
                        act.wait_ge(*V.after("gf"))
                        act.activation(t1[:, :], gf[:, :], ACT.Abs).then_inc(A.sem, 1)
                        act.wait_ge(*A.after("abs"))
                        act.activation(t1[:, :], t1[:, :], ACT.Exp, scale=-1.0).then_inc(A.sem, 1)
                        act.wait_ge(*A.after("exp"))
                        act.activation(t1[:, :], t1[:, :], ACT.Ln, bias=1.0).then_inc(A.sem, 1)
                        act.wait_ge(*V.after("mt"))
                        for c in range(TQ):
                            k = slice(c * P, (c + 1) * P)
                            act.activation(rows[:, 1, k], rows[:, 0, k], ACT.Exp, bias=mlast[:, c:c + 1]).then_inc(A.sem, 1)
                        for c in range(TQ):
                            k = slice(c * P, (c + 1) * P)
                            end = (c + 1) * P - 1
                            act.activation(t1[:, k], gi[:, k], ACT.Exp, bias=rows[:, 0, end:end + 1]).then_inc(A.sem, 1)
                        act.activation(rows[:, 2, :], rows[:, 2, :], ACT.Exp, scale=-1.0).then_inc(A.sem, 1)

                    @block.tensor
                    def _(pe):
                        pe.wait_ge(*V.after("a"))
                        for c in range(TQ):
                            last = pe.transpose(accA[0][:, c * HEADS:(c + 1) * HEADS], gi[:, c * P:(c + 1) * P],
                                                ident[0:HEADS, 0:HEADS])
                        last.then_inc(T.sem, 1)
                        pe.wait_ge(*A.after(f"wa{TQ - 1}"))
                        for c in range(TQ):
                            last = pe.transpose(accA[1][:, c * HEADS:(c + 1) * HEADS], t1[:, c * P:(c + 1) * P],
                                                ident[0:HEADS, 0:HEADS])
                        last.then_inc(T.sem, 1)

            with ExitStack() as g:
                wh = sb("head_w", [P, 3 * P], g)
                qT = sb("head_q", [P, S], g)
                kT = sb("head_k", [P, S], g)
                waV = sb("head_wav", [P, S], g)
                rowB = sb("head_rows", [P, 2, S], g)
                xst = sb("head_xstate", [P, TQ, 2 * P], g)
                aC = sb("head_a", [P, TQ], g)
                wC = sb("head_wa", [P, TQ], g)
                decay = sb("head_decay", [P, TQ], g)
                gs = sb("head_gain_skip", [P, 2], g)
                later = sb("head_later", [P, P], g)
                kn = stage[:, 0, :]
                vn = stage[:, 1, :]
                xmh = xst[:, 0:4, :].rearrange("p a b -> p (a b)")
                xch = xst[:, 4:8, :].rearrange("p a b -> p (a b)")
                free = sem("head_free")
                in_mask = sem("head_mask_landed")
                in_w = sem("head_w_landed")
                in_r = sem("head_rows_landed")
                in_e = sem("head_floor_landed")
                A = Steps(sem("head_act"), ["xm", "xc", "q", "k", "kn"] + [f"e{c}" for c in range(TQ)]
                          + ["abs", "sig", "sq", "root", "skip"])
                V = Steps(sem("head_dve"), ["a", "wa", "gs", "shift", "vn", "wav", "decay", "p", "qs"]
                          + [f"c{c}" for c in range(1, TQ)]
                          + ["floor", "rec", "num", "gated", "center", "rrec", "norm", "y"])
                T = Steps(sem("head_pe"), ["q", "k", "kn", "vn", "s", "u", "num", "mean", "var"])
                with nc.Block() as block:
                    @block.sync
                    def _(sp):
                        sp.dma_start(later[:, :], a["later"]).then_inc(in_mask, 16)
                        with sp.Fori(0, HEADS) as h:
                            sp.wait_ge(free, h + 1)
                            sp.dma_start(wh[:, :], a["w_qkv"][h]).then_inc(in_w, 16)
                            for n in range(2):
                                sp.dma_start(rowB[:, n, :], rows_d[h, n:n + 1, :].to_broadcast([P, S])).then_inc(in_r, 16)
                            sp.wait_ge(*V.after("qs", h))
                            sp.dma_start(rowB[:, 1, :], rows_d[h, 2:3, :].to_broadcast([P, S])).then_inc(in_e, 16)

                    @block.scalar
                    def _(act):
                        with act.Fori(0, HEADS) as h:
                            act.wait_ge(free, h + 1)
                            act.activation(xmh, at(pm, h), ACT.Copy).then_inc(A.sem, 1)
                            act.activation(xch, at(xcv, h), ACT.Copy).then_inc(A.sem, 1)
                            act.wait_ge(*T.after("q", h))
                            act.activation(qT[:, :], accA[0][:, :], ACT.Copy).then_inc(A.sem, 1)
                            act.wait_ge(*T.after("k", h))
                            act.activation(kT[:, :], accA[1][:, :], ACT.Copy, scale=SCALE).then_inc(A.sem, 1)
                            act.wait_ge(*T.after("kn", h))
                            act.activation(kn, accB[0][:, :], ACT.Copy, scale=SCALE).then_inc(A.sem, 1)
                            act.wait_ge(*V.after("shift", h))
                            for c in range(TQ):
                                k = slice(c * P, (c + 1) * P)
                                act.activation(rowB[:, 0, k], rowB[:, 0, k], ACT.Exp, bias=aC[:, c:c + 1]).then_inc(A.sem, 1)
                            act.wait_ge(*T.after("num", h))
                            act.activation(kT[:, :], accA[1][:, :], ACT.Abs).then_inc(A.sem, 1)
                            act.activation(waV[:, :], at(pm, h + HEADS), ACT.Sigmoid).then_inc(A.sem, 1)
                            act.wait_ge(*V.after("center", h))
                            act.activation(waV[:, :], qT[:, :], ACT.Square).then_inc(A.sem, 1)
                            act.wait_ge(*T.after("var", h))
                            act.activation(waV[:, :], accB[1][:, :], ACT.Sqrt, scale=1.0 / P, bias=eps[:, 0:1]).then_inc(A.sem, 1)
                            act.activation(kT[:, :], at(xcv, h), ACT.Copy, scale=gs[:, 1:2]).then_inc(A.sem, 1)

                    @block.vector
                    def _(dve):
                        dve.sem_inc(free, 1)
                        dve.wait_ge(in_mask, 16)
                        m0 = COLS["mnorm_skip"][0]
                        with dve.Fori(0, HEADS) as h:
                            dve.tensor_copy(aC[:, :], acol[:, :, bass.ds(h, 1)].rearrange("p c h -> p (c h)")).then_inc(V.sem, 1)
                            dve.tensor_copy(wC[:, :], wcol[:, :, bass.ds(h, 1)].rearrange("p c h -> p (c h)")).then_inc(V.sem, 1)
                            dve.tensor_copy(gs[:, :], col[:, bass.ds(h * 2 + m0, 2)]).then_inc(V.sem, 1)
                            dve.wait_ge(in_r, h * 32 + 32)
                            r0 = rowB[:, 0, :].rearrange("p (c t) -> p c t", t=P)
                            dve.tensor_tensor(r0, r0, later[:, :].unsqueeze(1).to_broadcast([P, TQ, P]), ALU.add).then_inc(V.sem, 1)
                            dve.wait_ge(*T.after("vn", h))
                            dve.tensor_copy(vn, accB[1][:, :]).then_inc(V.sem, 1)
                            dve.wait_ge(*V.after("vn", h))
                            dve.tensor_tensor(waV[:, :].rearrange("p (c v) -> p c v", v=P), vn.rearrange("p (c v) -> p c v", v=P),
                                              wC[:, :].unsqueeze(2).to_broadcast([P, TQ, P]), ALU.mult).then_inc(V.sem, 1)
                            r1 = rowB[:, 1, :].rearrange("p (c t) -> p c t", t=P)
                            dve.tensor_copy(decay[:, :].unsqueeze(2), r1[:, :, P - 1:P]).then_inc(V.sem, 1)
                            dve.wait_ge(*T.after("s", h))
                            dve.wait_ge(*A.after(f"e{TQ - 1}", h))
                            dve.tensor_tensor(rowB[:, 0, :], accA[0][:, :], rowB[:, 0, :], ALU.mult).then_inc(V.sem, 1)
                            dve.tensor_tensor(qT[:, :], qT[:, :], rowB[:, 1, :], ALU.mult).then_inc(V.sem, 1)
                            dve.wait_ge(*T.after("u", h))
                            for c in range(1, TQ):
                                u = accB[(c - 1) // 4][:, (c - 1) % 4 * 2 * P:((c - 1) % 4 + 1) * 2 * P]
                                if c == 1:
                                    dve.tensor_copy(xst[:, 1, :], u).then_inc(V.sem, 1)
                                else:
                                    dve.wait_ge(*V.after(f"c{c - 1}", h))
                                    dve.scalar_tensor_tensor(out=xst[:, c, :], in0=xst[:, c - 1, :], scalar=decay[:, c - 1:c],
                                                             in1=u, op0=ALU.mult, op1=ALU.add).then_inc(V.sem, 1)
                            dve.wait_ge(*A.after("abs", h))
                            dve.wait_ge(in_e, h * 16 + 16)
                            dve.tensor_tensor(kT[:, :], kT[:, :], rowB[:, 1, :], ALU.max).then_inc(V.sem, 1)
                            dve.wait_ge(*V.after("floor", h))
                            dve.reciprocal(kT[:, :], kT[:, :]).then_inc(V.sem, 1)
                            dve.wait_ge(*V.after("rec", h))
                            dve.tensor_tensor(qT[:, :], accA[0][:, :], kT[:, :], ALU.mult).then_inc(V.sem, 1)
                            dve.wait_ge(*A.after("sig", h))
                            dve.wait_ge(*V.after("num", h))
                            dve.tensor_tensor(qT[:, :], qT[:, :], waV[:, :], ALU.mult).then_inc(V.sem, 1)
                            dve.wait_ge(*T.after("mean", h))
                            dve.scalar_tensor_tensor(out=qT[:, :], in0=accB[0][:, :], scalar=-1.0 / P, in1=qT[:, :],
                                                     op0=ALU.mult, op1=ALU.add).then_inc(V.sem, 1)
                            dve.wait_ge(*A.after("root", h))
                            dve.reciprocal(waV[:, :], waV[:, :]).then_inc(V.sem, 1)
                            dve.wait_ge(*V.after("rrec", h))
                            dve.scalar_tensor_tensor(out=qT[:, :], in0=qT[:, :], scalar=gs[:, 0:1], in1=waV[:, :],
                                                     op0=ALU.mult, op1=ALU.mult).then_inc(V.sem, 1)
                            dve.wait_ge(*V.after("norm", h))
                            dve.wait_ge(*A.after("skip", h))
                            dve.tensor_tensor(at(pm, h + HEADS), qT[:, :], kT[:, :], ALU.add).then_inc(V.sem, 1)
                            dve.wait_ge(*V.after("y", h))
                            dve.sem_inc(free, 1)

                    @block.tensor
                    def _(pe):
                        with pe.Fori(0, HEADS) as h:
                            pe.wait_ge(in_w, h * 16 + 16)
                            pe.wait_ge(*A.after("xc", h))
                            for n, acc in ((0, accA[0]), (1, accA[1])):
                                for c0 in (0, BANK):
                                    last = pe.matmul(acc[:, c0:c0 + BANK], wh[:, n * P:(n + 1) * P],
                                                     xch[:, c0:c0 + BANK], start=True, stop=True)
                                last.then_inc(T.sem, 1)
                            for n, acc, src in ((1, accB[0], xch), (2, accB[1], xmh)):
                                for c in range(TQ):
                                    last = pe.matmul(acc[:, c * P:(c + 1) * P], src[:, c * P:(c + 1) * P],
                                                     wh[:, n * P:(n + 1) * P], start=True, stop=True)
                                last.then_inc(T.sem, 1)
                            pe.wait_ge(*A.after("k", h))
                            for c in range(TQ):
                                k = slice(c * P, (c + 1) * P)
                                last = pe.matmul(accA[0][:, k], kT[:, k], qT[:, k], start=True, stop=True)
                            last.then_inc(T.sem, 1)
                            pe.wait_ge(*A.after("kn", h))
                            pe.wait_ge(*V.after("wav", h))
                            for c in range(TQ - 1):
                                k = slice(c * P, (c + 1) * P)
                                u = accB[c // 4][:, c % 4 * 2 * P:(c % 4 + 1) * 2 * P]
                                pe.matmul(u[:, 0:P], kn[:, k], waV[:, k], start=True, stop=True)
                                last = pe.matmul(u[:, P:2 * P], kn[:, k], wC[:, c:c + 1].to_broadcast([P, P]),
                                                 start=True, stop=True)
                            last.then_inc(T.sem, 1)
                            pe.wait_ge(*V.after(f"c{TQ - 1}", h))
                            for c in range(TQ):
                                k = slice(c * P, (c + 1) * P)
                                pe.matmul(accA[0][:, k], vn[:, k], rowB[:, 0, k], start=True, stop=(c == 0))
                                if c:
                                    pe.matmul(accA[0][:, k], xst[:, c, 0:P], qT[:, k], start=False, stop=True)
                                last = pe.matmul(accA[1][:, k], ones[:, :], rowB[:, 0, k], start=True, stop=(c == 0))
                                if c:
                                    last = pe.matmul(accA[1][:, k], xst[:, c, P:2 * P], qT[:, k], start=False, stop=True)
                            last.then_inc(T.sem, 1)
                            pe.wait_ge(*V.after("gated", h))
                            for c0 in (0, BANK):
                                last = pe.matmul(accB[0][:, c0:c0 + BANK], ones[:, :], qT[:, c0:c0 + BANK], start=True, stop=True)
                            last.then_inc(T.sem, 1)
                            pe.wait_ge(*A.after("sq", h))
                            for c0 in (0, BANK):
                                last = pe.matmul(accB[1][:, c0:c0 + BANK], ones[:, :], waV[:, c0:c0 + BANK], start=True, stop=True)
                            last.then_inc(T.sem, 1)
        env["gate_and_project"](pm, HEADS, pm[:, 0, :], 2 * HEADS, 0)


def diff_mixer(nc, a, env):
    sem, col, ident, ones, eps, stage = (env[k] for k in ("sem", "col", "ident", "ones", "eps", "stage"))
    accA, accB = env["accA"], env["accB"]
    W = 2 * (P // 2)
    SCALE = float(P // 2) ** -0.5
    LAM0 = 0.8 - 0.6
    with ExitStack() as mix:
        pd = mix.enter_context(nc.sbuf_tensor("pd", [P, 3 * HEADS, S], F32))
        env["project"](pd, 12, 3 * HEADS)
        with ExitStack() as es:
            def sb(name, shape):
                return es.enter_context(nc.sbuf_tensor(name, shape, F32))
            lv = sb("lam_in", [P // 2, 4])
            lp = sb("lam_products", [P // 2, 2])
            le = sb("lam_exps", [P, 2])
            lam = sb("neg_lam", [P, 1])
            future = sb("diff_future", [P, P])
            in_l = sem("lam_landed")
            L = Steps(sem("lam_steps"), ["prod", "sum", "exp", "diff", "lam"])
            with nc.Block() as block:
                @block.sync
                def _(sp):
                    sp.dma_start(lv[:, :], a["lam"]).then_inc(in_l, 16)
                    sp.dma_start(future[:, :], a["future"]).then_inc(in_l, 16)

                @block.vector
                def _(dve):
                    dve.wait_ge(in_l, 32)
                    dve.tensor_tensor(lp[:, :], lv[:, 0:2], lv[:, 2:4], ALU.mult).then_inc(L.sem, 1)
                    dve.wait_ge(*L.after("exp"))
                    dve.tensor_tensor(lam[:, :], le[:, 1:2], le[:, 0:1], ALU.subtract).then_inc(L.sem, 1)
                    dve.wait_ge(*L.after("diff"))
                    dve.tensor_scalar(lam[:, :], lam[:, :], LAM0, None, ALU.subtract).then_inc(L.sem, 1)

                @block.tensor
                def _(pe):
                    pe.wait_ge(*L.after("prod"))
                    pe.matmul(accA[0][:, 0:2], ones[0:P // 2, :], lp[:, :], start=True, stop=True).then_inc(L.sem, 1)

                @block.scalar
                def _(act):
                    act.wait_ge(*L.after("sum"))
                    act.activation(le[:, :], accA[0][:, 0:2], ACT.Exp).then_inc(L.sem, 1)

            qh = sb("diff_q", [P, S])
            kh = sb("diff_k", [P, S])
            pr = [sb(f"diff_p{m}", [P, S]) for m in range(2)]
            pt = sb("diff_pt", [P, S])
            vn = stage[:, 0, :]
            vh = stage[:, 1, :]
            mx = sb("diff_max", [P, 2])
            rs = sb("diff_sum", [P, 2])
            gd = sb("diff_gain", [P, 1])
            free = sem("diff_free")
            A = Steps(sem("diff_act"), ["q", "k", "v", "vn"] + [x for j in range(TQ) for x in (f"e{j}0", f"e{j}1", f"pt{j}")]
                      + ["sq", "od", "root"])
            V = Steps(sem("diff_dve"), ["gd0", "gd"] + [x for j in range(TQ) for x in
                      (f"mask{j}0", f"mask{j}1", f"max{j}0", f"max{j}1", f"neg{j}", f"rec{j}", f"nl{j}", f"p{j}0", f"p{j}1")]
                      + ["rrec", "y"])
            T = Steps(sem("diff_pe"), ["v"] + [f"s{j}{m}" for j in (0,) for m in range(2)]
                      + [x for j in range(TQ) for x in ([f"s{j + 1}0", f"s{j + 1}1"] if j + 1 < TQ else []) + [f"t{j}", f"o{j}"]]
                      + ["sum"])
            with nc.Block() as block:
                @block.scalar
                def _(act):
                    with act.Fori(0, HEADS) as h:
                        act.wait_ge(free, h + 1)
                        act.activation(qh[:, :], at(pd, h), ACT.Copy).then_inc(A.sem, 1)
                        act.activation(kh[:, :], at(pd, h + HEADS), ACT.Copy).then_inc(A.sem, 1)
                        act.activation(vh, at(pd, h + 2 * HEADS), ACT.Copy).then_inc(A.sem, 1)
                        act.wait_ge(*T.after("v", h))
                        act.activation(vn, accA[0][:, :], ACT.Copy).then_inc(A.sem, 1)
                        for j in range(TQ):
                            n = (j + 1) * P
                            for m in range(2):
                                act.wait_ge(*V.after(f"neg{j}", h))
                                if j:
                                    act.wait_ge(*T.after(f"t{j - 1}", h))
                                act.activation(pr[m][:, 0:n], accB[m][:, 0:n], ACT.Exp, scale=SCALE, bias=mx[:, m:m + 1],
                                               accum_out=rs[:, m:m + 1]).then_inc(A.sem, 1)
                            act.wait_ge(*T.after(f"t{j}", h))
                            if j:
                                act.wait_ge(*T.after(f"o{j - 1}", h))
                            act.activation(pt[:, 0:n], accA[0][:, 0:n], ACT.Copy).then_inc(A.sem, 1)
                        act.wait_ge(*T.after(f"o{TQ - 1}", h))
                        act.activation(kh[:, :], accA[1][:, :], ACT.Square).then_inc(A.sem, 1)
                        act.activation(qh[:, :], accA[1][:, :], ACT.Copy).then_inc(A.sem, 1)
                        act.wait_ge(*T.after("sum", h))
                        act.activation(pr[1][:, :], accA[0][:, :], ACT.Sqrt, scale=1.0 / W, bias=eps[:, 0:1]).then_inc(A.sem, 1)

                @block.vector
                def _(dve):
                    dve.sem_inc(free, 1)
                    d0 = COLS["dnorm_g"][0]
                    with dve.Fori(0, HEADS) as h:
                        dve.tensor_copy(gd[:, :], col[:, bass.ds(h + d0, 1)]).then_inc(V.sem, 1)
                        dve.wait_ge(*V.after("gd0", h))
                        dve.tensor_scalar(gd[:, :], gd[:, :], 1.0 - LAM0, None, ALU.mult).then_inc(V.sem, 1)
                        for j in range(TQ):
                            n = (j + 1) * P
                            for m in range(2):
                                dve.wait_ge(*T.after(f"s{j}{m}", h))
                                s_d = accB[m][:, j * P:n]
                                dve.tensor_tensor(s_d, s_d, future[:, :], ALU.add).then_inc(V.sem, 1)
                            for m in range(2):
                                dve.wait_ge(*V.after(f"mask{j}{m}", h))
                                dve.reduce_max(mx[:, m:m + 1], accB[m][:, 0:n], AX.X).then_inc(V.sem, 1)
                            dve.wait_ge(*V.after(f"max{j}1", h))
                            dve.tensor_scalar(mx[:, :], mx[:, :], -SCALE, None, ALU.mult).then_inc(V.sem, 1)
                            dve.wait_ge(*A.after(f"e{j}1", h))
                            dve.reciprocal(rs[:, :], rs[:, :]).then_inc(V.sem, 1)
                            dve.wait_ge(*V.after(f"rec{j}", h))
                            dve.tensor_tensor(rs[:, 1:2], rs[:, 1:2], lam[:, :], ALU.mult).then_inc(V.sem, 1)
                            dve.tensor_scalar(pr[0][:, 0:n], pr[0][:, 0:n], rs[:, 0:1], None, ALU.mult).then_inc(V.sem, 1)
                            dve.wait_ge(*V.after(f"p{j}0", h))
                            dve.scalar_tensor_tensor(out=pr[0][:, 0:n], in0=pr[1][:, 0:n], scalar=rs[:, 1:2],
                                                     in1=pr[0][:, 0:n], op0=ALU.mult, op1=ALU.add).then_inc(V.sem, 1)
                        dve.wait_ge(*A.after("root", h))
                        dve.reciprocal(pr[1][:, :], pr[1][:, :]).then_inc(V.sem, 1)
                        dve.wait_ge(*V.after("rrec", h))
                        dve.scalar_tensor_tensor(out=at(pd, h + 2 * HEADS), in0=qh[:, :], scalar=gd[:, 0:1],
                                                 in1=pr[1][:, :], op0=ALU.mult, op1=ALU.mult).then_inc(V.sem, 1)
                        dve.wait_ge(*V.after("y", h))
                        dve.sem_inc(free, 1)

                @block.tensor
                def _(pe):
                    with pe.Fori(0, HEADS) as h:
                        pe.wait_ge(*A.after("v", h))
                        for c in range(TQ):
                            last = pe.transpose(accA[0][:, c * P:(c + 1) * P], vh[:, c * P:(c + 1) * P], ident[:, :])
                        last.then_inc(T.sem, 1)
                        pe.wait_ge(*A.after("vn", h))

                        def scores(j):
                            n = (j + 1) * P
                            if j:
                                pe.wait_ge(*A.after(f"e{j - 1}1", h))
                            for m in range(2):
                                r = slice(m * (P // 2), (m + 1) * (P // 2))
                                for c0 in range(0, n, BANK):
                                    c1 = min(n, c0 + BANK)
                                    last = pe.matmul(accB[m][:, c0:c1], qh[r, j * P:n], kh[r, c0:c1], start=True, stop=True)
                                last.then_inc(T.sem, 1)
                        scores(0)
                        for j in range(TQ):
                            if j + 1 < TQ:
                                scores(j + 1)
                            pe.wait_ge(*V.after(f"p{j}1", h))
                            if j:
                                pe.wait_ge(*A.after(f"pt{j - 1}", h))
                            for c in range(j + 1):
                                last = pe.transpose(accA[0][:, c * P:(c + 1) * P], pr[0][:, c * P:(c + 1) * P], ident[:, :])
                            last.then_inc(T.sem, 1)
                            pe.wait_ge(*A.after(f"pt{j}", h))
                            for c in range(j + 1):
                                last = pe.matmul(accA[1][:, j * P:(j + 1) * P], vn[:, c * P:(c + 1) * P],
                                                 pt[:, c * P:(c + 1) * P], start=(c == 0), stop=(c == j))
                            last.then_inc(T.sem, 1)
                        pe.wait_ge(*A.after("sq", h))
                        for c0 in (0, BANK):
                            last = pe.matmul(accA[0][:, c0:c0 + BANK], ones[:, :], kh[:, c0:c0 + BANK], start=True, stop=True)
                        last.then_inc(T.sem, 1)
        env["gate_and_project"](pd, 2 * HEADS, pd[:, 0, :], 24, 1)


def memory_mixer(nc, a, env):
    sem, col, ident, ones, eps, stage = (env[k] for k in ("sem", "col", "ident", "ones", "eps", "stage"))
    accA, accB = env["accA"], env["accB"]
    tile_done = env["tile_done"]
    SCALE = float(P) ** -0.5
    MB = MEM // P
    with ExitStack() as mix:
        pc = mix.enter_context(nc.sbuf_tensor("pc", [P, HEADS, S], F32))
        env["project"](pc, 28, HEADS)
        with ExitStack() as es:
            def sb(name, shape, dt=F32, where=es):
                return where.enter_context(nc.sbuf_tensor(name, shape, dt))
            km = sb("mem_k", [P, HEADS, MEM])
            vT = sb("mem_vT", [P, HEADS, MEM])
            vn = sb("mem_v", [P, MB, HEADS * P])
            with ExitStack() as g:
                mT = sb("memT", [P, KD, MEM], F32, g)
                mH = sb("memH", [P, KD, MEM], F32R, g)
                mL = sb("memL", [P, KD, MEM], F32R, g)
                in_m = sem("mem_landed")
                with nc.Block() as block:
                    @block.sync
                    def _(sp):
                        sp.dma_start(mT[:, :, :], a["memT"].rearrange("(k p) s -> p k s", p=P)).then_inc(in_m, 16)
                        sp.wait_ge(in_m, 16)
                env["norm"](lambda k: mT[:, k, :], MEM, lambda k: env["c_"]("mem_norm_g", k), None,
                            hi=lambda k: mH[:, k, :], lo=lambda k: mL[:, k, :])

                def copy_mem(dst, p):
                    def epi(act, i, done, acc, psum_free):
                        act.wait_ge(tile_done, done)
                        act.activation(at(dst, i * 2 + p), acc[:, 0:MEM], ACT.Copy).then_inc(psum_free, 1)
                    return epi
                with nc.Block() as block:
                    env["weight_stream"]([
                        dict(w=a["w_mem_kv"][n * HEADS:(n + 1) * HEADS], K=KD, iters=HEADS // 2,
                             act=[copy_mem(dst, 0), copy_mem(dst, 1)], dve=[None, None],
                             rhs=lambda q, k: (mH, mL)[q][:, k, :], cols=MEM, ready=None)
                        for n, dst in ((0, km), (1, vT))], block)
            tr = sem("mem_v_transposed")
            ev = sem("mem_v_copied")
            with nc.Block() as block:
                @block.tensor
                def _(pe):
                    for h in range(HEADS):
                        for b in range(MB):
                            last = pe.transpose(accA[b][:, h * P:(h + 1) * P], vT[:, h, b * P:(b + 1) * P], ident[:, :])
                    last.then_inc(tr, 1)

                @block.vector
                def _(dve):
                    dve.wait_ge(tr, 1)
                    for b in range(MB):
                        dve.tensor_copy(vn[:, b, :], accA[b][:, 0:HEADS * P]).then_inc(ev, 1)

            qh = sb("mem_q", [P, S])
            vh = sb("mem_v_head", [P, MB, P])
            pm = sb("mem_p", [P, TQ, MEM])
            pt = sb("mem_pt", [P, MB, S])
            mx = sb("mem_max", [P, TQ])
            rs = sb("mem_sum", [P, TQ])
            free = sem("mem_free")
            A = Steps(sem("mem_act"), ["q"] + [f"e{j}" for j in range(TQ)] + ["pt0"])
            V = Steps(sem("mem_dve"), ["v", "max0", "max1", "neg", "rec", "p", "pt1", "o"])
            T = Steps(sem("mem_pe"), ["s0", "s1", "t0", "t1", "o"])
            with nc.Block() as block:
                @block.scalar
                def _(act):
                    act.sem_inc(free, 1)
                    with act.Fori(0, HEADS) as h:
                        act.wait_ge(free, h + 1)
                        act.activation(qh[:, :], at(pc, h), ACT.Copy).then_inc(A.sem, 1)
                        act.wait_ge(*V.after("neg", h))
                        for j in range(TQ):
                            act.activation(pm[:, j, :], accB[j // 4][:, j % 4 * MEM:(j % 4 + 1) * MEM], ACT.Exp, scale=SCALE,
                                           bias=mx[:, j:j + 1], accum_out=rs[:, j:j + 1]).then_inc(A.sem, 1)
                        act.wait_ge(*T.after("t0", h))
                        act.activation(pt[:, 0, :], accA[0][:, :], ACT.Copy).then_inc(A.sem, 1)

                @block.vector
                def _(dve):
                    with dve.Fori(0, HEADS) as h:
                        dve.wait_ge(free, h + 1)
                        dve.tensor_copy(vh[:, :, :], vn[:, :, bass.ds(h * P, P)]).then_inc(V.sem, 1)
                        for n in range(2):
                            dve.wait_ge(*T.after(f"s{n}", h))
                            dve.reduce_max(mx[:, n * 4:n * 4 + 4], accB[n][:, :].rearrange("p (j m) -> p j m", m=MEM),
                                           AX.X).then_inc(V.sem, 1)
                        dve.wait_ge(*V.after("max1", h))
                        dve.tensor_scalar(mx[:, :], mx[:, :], -SCALE, None, ALU.mult).then_inc(V.sem, 1)
                        dve.wait_ge(*A.after(f"e{TQ - 1}", h))
                        dve.reciprocal(rs[:, :], rs[:, :]).then_inc(V.sem, 1)
                        dve.wait_ge(*V.after("rec", h))
                        dve.tensor_tensor(pm[:, :, :], pm[:, :, :], rs[:, :].unsqueeze(2).to_broadcast([P, TQ, MEM]),
                                          ALU.mult).then_inc(V.sem, 1)
                        dve.wait_ge(*T.after("t1", h))
                        dve.tensor_copy(pt[:, 1, :], accA[1][:, :]).then_inc(V.sem, 1)
                        dve.wait_ge(*T.after("o", h))
                        dve.tensor_scalar(at(pc, h), accB[0][:, :], 1.0, None, ALU.mult).then_inc(V.sem, 1)
                        dve.wait_ge(*V.after("o", h))
                        dve.sem_inc(free, 1)

                @block.tensor
                def _(pe):
                    with pe.Fori(0, HEADS) as h:
                        pe.wait_ge(*A.after("q", h))
                        for j in range(TQ):
                            last = pe.matmul(accB[j // 4][:, j % 4 * MEM:(j % 4 + 1) * MEM], qh[:, j * P:(j + 1) * P],
                                             flat(km[:, bass.ds(h, 1), :]), start=True, stop=True)
                            if j % 4 == 3:
                                last.then_inc(T.sem, 1)
                        pe.wait_ge(*V.after("p", h))
                        for b in range(MB):
                            for j in range(TQ):
                                last = pe.transpose(accA[b][:, j * P:(j + 1) * P], pm[:, j, b * P:(b + 1) * P], ident[:, :])
                            last.then_inc(T.sem, 1)
                        pe.wait_ge(*A.after("pt0", h))
                        pe.wait_ge(*V.after("pt1", h))
                        for c0 in (0, BANK):
                            for b in range(MB):
                                last = pe.matmul(accB[0][:, c0:c0 + BANK], vh[:, b, :], pt[:, b, c0:c0 + BANK],
                                                 start=(b == 0), stop=(b == MB - 1))
                        last.then_inc(T.sem, 1)
        _memory_out(nc, env, pc)


def _memory_out(nc, env, pc):
    with ExitStack() as es:
        sz = es.enter_context(nc.sbuf_tensor("mem_silu", [P, S], F32))
        env["gate_and_project"](pc, 0, sz[:, :], 32, 2)


def by_step(t):
    return t.rearrange("p (j c) -> p c j", j=STEP)


def second_block(nc, a, env):
    mods, gain, xT = env["mods"], env["gain"], env["xT"]

    def modulated_norm(which, layer, part, bufs=None, **where):
        if bufs is not None:
            return env["norm_programs"](bufs, lambda k: xT[:, k, :], S, lambda k: gain[:, which * KD + k:which * KD + k + 1],
                                        lambda k: mods[:, layer * 48 + part * KD + k:layer * 48 + part * KD + k + 1], **where)
        env["norm"](lambda k: xT[:, k, :], S, lambda k: gain[:, which * KD + k:which * KD + k + 1],
                    lambda k: mods[:, layer * 48 + part * KD + k:layer * 48 + part * KD + k + 1], **where)
    env["modulated_norm"] = modulated_norm
    for layer, mixer in enumerate((s5_mixer, conv_mixer)):
        mixer(nc, a, env, layer)
        if env["stage_end"](f"mix{layer}"):
            return
        swiglu(nc, a, env, layer)
        if env["stage_end"](f"ffn{layer}"):
            return


def s5_mixer(nc, a, env, layer):
    sem, col, ident, xT, mods = (env[k] for k in ("sem", "col", "ident", "xT", "mods"))
    accA, accB = env["accA"], env["accB"]
    tile_done = env["tile_done"]
    NG = 2 * QPAIRS
    h_d = nc.dram_tensor("s5_in", [D, STEP, NSTEP], F32).ap()
    y_d = nc.dram_tensor("s5_out", [D, STEP, NSTEP], F32).ap()
    k_d = nc.dram_tensor("s5_kernel", [GROUP_W, NG, 2 * P - GROUP_W], F32).ap()
    LO = P - GROUP_W
    with ExitStack() as outer:
        hf = outer.enter_context(nc.sbuf_tensor("s5_h", [P, KD, S], F32))
        env["modulated_norm"](0, layer, 0, full=lambda k: by_step(hf[:, k, :]), steps=True)
        h_out = sem("s5_h_stored")
        with nc.Block() as block:
            @block.sync
            def _(sp):
                sp.dma_start(h_d.rearrange("(k p) j c -> p k (j c)", p=P), hf[:, :, :]).then_inc(h_out, 16)
                sp.wait_ge(h_out, 16)

        with ExitStack() as es:
            def sb(name, shape):
                return es.enter_context(nc.sbuf_tensor("s5_" + name, shape, F32))
            prm = sb("prm", [P, 3, QPAIRS])
            bc = sb("bc", [P, 4, QPAIRS * GROUP_W])
            step_no = sb("step_no", [P, NSTEP])
            v = sb("v", [P, 24, QPAIRS])
            pwr = sb("pwr", [P, QPAIRS, STEP + 1])
            pwi = sb("pwi", [P, QPAIRS, STEP + 1])
            bb = sb("bbar", [P, 2, QPAIRS * GROUP_W])
            tb = sb("tb", [P, 2, QPAIRS * GROUP_W])
            NCA = QPAIRS * (STEP + 1) * GROUP_W
            ca = sb("ca", [P, 2, NCA])
            tca = sb("tca", [P, 2, NCA])
            ab = sb("ab", [P, 2, QPAIRS * P])
            G = sb("g", [P, 2, QPAIRS * P])
            U = sb("u", [P, NG, NSTEP])
            Tz = sb("toeplitz", [P, NG, P])
            kp = sb("kpad", [GROUP_W, QPAIRS, 2, 2 * P - GROUP_W])
            cs = sb("cos", [P, QPAIRS * NSTEP])
            sn = sb("sin", [P, QPAIRS * NSTEP])
            rt = sb("modulus", [P, QPAIRS * NSTEP])
            z = [sb(f"z{n}", [P, QPAIRS * NSTEP]) for n in range(2)]
            t = [sb(f"t{n}", [P, QPAIRS * NSTEP]) for n in range(2)]
            Y = sb("y", [P, QPAIRS, 2, NSTEP])

            free = sem("s5_pass_free")
            in_c = sem("s5_steps_landed")
            in_p = sem("s5_params_landed")
            in_u = sem("s5_u_landed")
            k_out = sem("s5_kernel_stored")
            in_t = sem("s5_toeplitz_landed")
            y_out = sem("s5_y_stored")
            kz = sem("s5_kpad_zeroed")
            chain = sem("s5_dve_chain")
            LINKS = 123
            R = Steps(sem("s5_ready"), ["x", "angle", "phase", "ab", "ca", "gim", "kodd", "z", "yodd"])
            A = Steps(sem("s5_act"), ["dt", "mag", "r8", "sin", "cos", "tsin", "tcos", "gre", "keven", "yeven"])
            T = Steps(sem("s5_pe"), ["g", "k", "v", "y"])
            q_n = {n: i for i, n in enumerate(("lr", "dt", "x", "ang", "turns", "r", "r2", "mag", "sin", "cos", "r8",
                                               "den", "am1", "t0", "t1", "qr", "qi", "phi", "lim"))}

            def w(name):
                return v[:, q_n[name], :]

            def b16(x):
                return x.unsqueeze(2).to_broadcast([P, QPAIRS, GROUP_W])

            def m16(x):
                return x.rearrange("p (q h) -> p q h", h=GROUP_W)

            with nc.Block() as block:
                @block.sync
                def _(sp):
                    sp.dma_start(step_no[:, :], a["step_no"]).then_inc(in_c, 16)
                    with sp.Fori(0, PASSES) as r:
                        sp.wait_ge(free, r + 1)
                        sp.dma_start(prm[:, :, :], a["ssm_a"][r]).then_inc(in_p, 16)
                        sp.dma_start(bc[:, :, :], a["ssm_bc"][r]).then_inc(in_p, 16)
                        src = h_d.rearrange("(g h) j c -> j h g c", h=GROUP_W)
                        for n in range(STEP):
                            sp.dma_start(U[n * GROUP_W:(n + 1) * GROUP_W, :, :],
                                         src[STEP - 1 - n, :, bass.ds(r * NG, NG), :]).then_inc(in_u, 16)
                        sp.wait_ge(*A.after("keven", r))
                        sp.wait_ge(*R.after("kodd", r))
                        sp.dma_start(k_d.rearrange("h g c -> h (g c)"), kp[:, :, :, :].rearrange("h q e c -> h (q e c)")
                                     ).then_inc(k_out, 16)
                        sp.wait_ge(k_out, r * 16 + 16)
                        for n in range(STEP):
                            sp.dma_start(Tz[n * GROUP_W:(n + 1) * GROUP_W, :, :],
                                         k_d[:, :, n * GROUP_W:n * GROUP_W + P]).then_inc(in_t, 16)
                        sp.wait_ge(y_out, r * (16 * STEP) + 16 * STEP)
                        sp.sem_inc(free, 1)

                @block.scalar
                def _(act):
                    with act.Fori(0, PASSES) as r:
                        act.wait_ge(in_p, r * 32 + 32)
                        act.activation(w("dt"), prm[:, 2, :], ACT.Exp).then_inc(A.sem, 1)
                        act.wait_ge(*R.after("x", r))
                        act.activation(w("mag"), w("x"), ACT.Exp).then_inc(A.sem, 1)
                        act.activation(w("r8"), w("x"), ACT.Exp, scale=float(STEP)).then_inc(A.sem, 1)
                        act.wait_ge(*R.after("angle", r))
                        act.activation(w("sin"), w("r"), ACT.Sin).then_inc(A.sem, 1)
                        act.activation(w("cos"), w("r2"), ACT.Sin).then_inc(A.sem, 1)
                        act.wait_ge(*R.after("phase", r))
                        act.activation(sn[:, :], t[0][:, :], ACT.Sin).then_inc(A.sem, 1)
                        act.activation(cs[:, :], t[1][:, :], ACT.Sin).then_inc(A.sem, 1)
                        act.wait_ge(*T.after("g", r))
                        act.activation(G[:, 0, :], accA[0][:, :], ACT.Copy).then_inc(A.sem, 1)
                        act.wait_ge(*T.after("k", r))
                        act.activation(kp[:, :, 0, LO:], accB[0][0:GROUP_W, :].rearrange("h (q c) -> h q c", c=P),
                                       ACT.Copy).then_inc(A.sem, 1)
                        act.wait_ge(*T.after("y", r))
                        act.activation(Y[:, :, 0, :], accB[0][:, :].rearrange("p (q c) -> p q c", c=NSTEP),
                                       ACT.Copy).then_inc(A.sem, 1)
                        act.wait_ge(*A.after("yeven", r))
                        act.wait_ge(*R.after("yodd", r))
                        dst = y_d.rearrange("(g h) j c -> j h g c", h=GROUP_W)
                        for j in range(STEP):
                            act.dma_start(dst[j, :, bass.ds(r * NG, NG), :],
                                          Y[j * GROUP_W:(j + 1) * GROUP_W, :, :, :].rearrange("h q e c -> h (q e) c")
                                          ).then_inc(y_out, 16)

                @block.vector
                def _(dve):
                    dve.memset(kp[:, :, :, :], 0.0).then_inc(kz, 1)
                    dve.wait_ge(kz, 1)
                    dve.wait_ge(in_c, 16)
                    dve.sem_inc(free, 1)
                    with dve.Fori(0, PASSES) as r:
                        n = [0]

                        def link(ins):
                            n[0] += 1
                            ins.then_inc(chain, 1)
                            dve.wait_ge(chain, r * LINKS + n[0])

                        def ready(name):
                            dve.sem_inc(R.sem, 1)

                        def tt(o, x, y, op):
                            link(dve.tensor_tensor(o, x, y, op))

                        def ts(o, x, s1, op1, s2=None, op2=None):
                            if op2 is None:
                                link(dve.tensor_scalar(o, x, s1, None, op1))
                            else:
                                link(dve.tensor_scalar(o, x, s1, s2, op1, op2))

                        def stt(o, x, s1, y, op1, op2):
                            link(dve.scalar_tensor_tensor(out=o, in0=x, scalar=s1, in1=y, op0=op1, op1=op2))

                        def turn(x, turns, quarter):
                            ts(turns, x, 1.0 / TWO_PI, ALU.mult)
                            ts(turns, turns, 12582912.0, ALU.add, 12582912.0, ALU.subtract)
                            stt(x, turns, -6.28125, x, ALU.mult, ALU.add)
                            stt(x, turns, -(TWO_PI - 6.28125), x, ALU.mult, ALU.add)
                            if quarter is not None:
                                ts(quarter, x, TWO_PI / 4, ALU.add)
                                ts(turns, quarter, TWO_PI / 2, ALU.is_gt, -TWO_PI, ALU.mult)
                                tt(quarter, quarter, turns, ALU.add)
                                ts(quarter, quarter, 3.1415925, ALU.min, -3.1415925, ALU.max)
                                ts(x, x, 3.1415925, ALU.min, -3.1415925, ALU.max)

                        dve.wait_ge(free, r + 1)
                        dve.wait_ge(in_p, r * 32 + 32)
                        ts(w("lr"), prm[:, 0, :], -1e-4, ALU.min)
                        dve.wait_ge(*A.after("dt", r))
                        tt(w("x"), w("lr"), w("dt"), ALU.mult)
                        ready("x")
                        tt(w("r"), prm[:, 1, :], w("dt"), ALU.mult)
                        turn(w("r"), w("turns"), w("r2"))
                        ready("angle")
                        ts(w("phi"), w("r"), float(STEP), ALU.mult)
                        turn(w("phi"), w("turns"), None)
                        q3 = lambda x: x.rearrange("p (q c) -> p q c", c=NSTEP)
                        tt(q3(t[0][:, :]), w("phi").unsqueeze(2).to_broadcast([P, QPAIRS, NSTEP]),
                           step_no[:, :].unsqueeze(1).to_broadcast([P, QPAIRS, NSTEP]), ALU.mult)
                        turn(t[0][:, :], z[0][:, :], t[1][:, :])
                        ready("phase")
                        dve.wait_ge(*A.after("cos", r))
                        link(dve.tensor_copy(q3(rt[:, :]), w("r8").unsqueeze(2).to_broadcast([P, QPAIRS, NSTEP])))
                        link(dve.memset(q3(rt[:, :])[:, :, 0:1], 0.0))
                        link(dve.memset(pwr[:, :, 0:1], 1.0))
                        link(dve.memset(pwi[:, :, 0:1], 0.0))
                        p1 = (pwr[:, :, 1:2].rearrange("p q n -> p (q n)"), pwi[:, :, 1:2].rearrange("p q n -> p (q n)"))
                        tt(p1[0], w("mag"), w("cos"), ALU.mult)
                        tt(p1[1], w("mag"), w("sin"), ALU.mult)
                        tt(w("den"), w("lr"), w("lr"), ALU.mult)
                        tt(w("t0"), prm[:, 1, :], prm[:, 1, :], ALU.mult)
                        tt(w("den"), w("den"), w("t0"), ALU.add)
                        link(dve.reciprocal(w("den"), w("den")))
                        ts(w("am1"), p1[0], -1.0, ALU.add)
                        tt(w("t0"), w("am1"), w("lr"), ALU.mult)
                        tt(w("t1"), p1[1], prm[:, 1, :], ALU.mult)
                        tt(w("t0"), w("t0"), w("t1"), ALU.add)
                        tt(w("qr"), w("t0"), w("den"), ALU.mult)
                        tt(w("t0"), p1[1], w("lr"), ALU.mult)
                        tt(w("t1"), w("am1"), prm[:, 1, :], ALU.mult)
                        tt(w("t0"), w("t0"), w("t1"), ALU.subtract)
                        tt(w("qi"), w("t0"), w("den"), ALU.mult)

                        def times(o, re, im, xre, xim, tmp, minus_im=False):
                            tt(tmp[0], re, xre, ALU.mult)
                            tt(tmp[1], im, xim, ALU.mult)
                            tt(o[0], tmp[0], tmp[1], ALU.subtract)
                            tt(tmp[0], re, xim, ALU.mult)
                            tt(tmp[1], im, xre, ALU.mult)
                            if minus_im:
                                link(dve.scalar_tensor_tensor(out=o[2], in0=o[3], scalar=-1.0, in1=o[4],
                                                              op0=ALU.mult, op1=ALU.subtract))
                            else:
                                tt(o[1], tmp[0], tmp[1], ALU.add)

                        times((m16(bb[:, 0, :]), m16(bb[:, 1, :])), b16(w("qr")), b16(w("qi")), m16(bc[:, 0, :]),
                              m16(bc[:, 1, :]), (m16(tb[:, 0, :]), m16(tb[:, 1, :])))
                        for e in range(2, STEP + 1):
                            pn = lambda x, e: x[:, :, e:e + 1].rearrange("p q n -> p (q n)")
                            times((pn(pwr, e), pn(pwi, e)), pn(pwr, e - 1), pn(pwi, e - 1), p1[0], p1[1], (w("t0"), w("t1")))

                        def powers(x, n_):
                            return x[:, :, 0:n_].unsqueeze(3).to_broadcast([P, QPAIRS, n_, GROUP_W])

                        def over(x, n_):
                            return m16(x).unsqueeze(2).to_broadcast([P, QPAIRS, n_, GROUP_W])

                        def q4(x, n_):
                            return x.rearrange("p (q n h) -> p q n h", n=n_, h=GROUP_W)
                        times([q4(ab[:, i, :], STEP) for i in range(2)], powers(pwr, STEP), powers(pwi, STEP),
                              over(bb[:, 0, :], STEP), over(bb[:, 1, :], STEP),
                              [q4(tca[:, i, 0:QPAIRS * P], STEP) for i in range(2)])
                        ready("ab")
                        times([q4(ca[:, 0, :], STEP + 1), None, ca[:, 1, :], tca[:, 0, :], tca[:, 1, :]],
                              powers(pwr, STEP + 1), powers(pwi, STEP + 1), over(bc[:, 2, :], STEP + 1),
                              over(bc[:, 3, :], STEP + 1), [q4(tca[:, i, :], STEP + 1) for i in range(2)], minus_im=True)
                        ready("ca")
                        dve.wait_ge(*T.after("g", r))
                        link(dve.tensor_copy(G[:, 1, :], accA[1][:, :]))
                        ready("gim")
                        dve.wait_ge(*T.after("k", r))
                        link(dve.tensor_copy(kp[:, :, 1, LO:], accB[1][0:GROUP_W, :].rearrange("h (q c) -> h q c", c=P)))
                        ready("kodd")
                        dve.wait_ge(*T.after("v", r))
                        dve.wait_ge(*A.after("tcos", r))
                        tt(t[0][:, :], accA[0][:, :], cs[:, :], ALU.mult)
                        tt(t[1][:, :], accA[1][:, :], sn[:, :], ALU.mult)
                        tt(z[0][:, :], t[0][:, :], t[1][:, :], ALU.add)
                        tt(t[0][:, :], accA[1][:, :], cs[:, :], ALU.mult)
                        tt(t[1][:, :], accA[0][:, :], sn[:, :], ALU.mult)
                        tt(z[1][:, :], t[0][:, :], t[1][:, :], ALU.subtract)
                        link(dve.tensor_tensor_scan(t[0][:, :], rt[:, :], z[0][:, :], 0.0, ALU.mult, ALU.add))
                        link(dve.tensor_tensor_scan(t[1][:, :], rt[:, :], z[1][:, :], 0.0, ALU.mult, ALU.add))
                        tt(z[0][:, :], t[0][:, :], cs[:, :], ALU.mult)
                        tt(rt[:, :], t[1][:, :], sn[:, :], ALU.mult)
                        tt(z[0][:, :], z[0][:, :], rt[:, :], ALU.subtract)
                        tt(z[1][:, :], t[1][:, :], cs[:, :], ALU.mult)
                        tt(rt[:, :], t[0][:, :], sn[:, :], ALU.mult)
                        tt(z[1][:, :], z[1][:, :], rt[:, :], ALU.add)
                        ready("z")
                        dve.wait_ge(*T.after("y", r))
                        link(dve.tensor_copy(Y[:, :, 1, :], accB[1][:, :].rearrange("p (q c) -> p q c", c=NSTEP)))
                        ready("yodd")
                        assert n[0] == LINKS, n[0]

                @block.tensor
                def _(pe):
                    HALF = P // 2
                    with pe.Fori(0, PASSES) as r:
                        pe.wait_ge(*R.after("ca", r))
                        for i in range(2):
                            for q in range(QPAIRS):
                                last = pe.transpose(accA[i][:, q * P:(q + 1) * P], ab[:, i, q * P:(q + 1) * P], ident[:, :])
                        last.then_inc(T.sem, 1)
                        NQ = (STEP + 1) * GROUP_W
                        for q in range(QPAIRS):
                            for e in range(2):
                                rows = slice(e * HALF, (e + 1) * HALF)
                                for i in range(2):
                                    last = pe.matmul(accB[e][0:GROUP_W, q * P:(q + 1) * P],
                                                     bb[rows, i, q * GROUP_W:(q + 1) * GROUP_W],
                                                     ca[rows, i, q * NQ:q * NQ + P], start=(i == 0), stop=(i == 1))
                        last.then_inc(T.sem, 1)
                        pe.wait_ge(in_u, r * (16 * STEP) + 16 * STEP)
                        pe.wait_ge(*A.after("gre", r))
                        pe.wait_ge(*R.after("gim", r))
                        for i in range(2):
                            for q in range(QPAIRS):
                                for e in range(2):
                                    last = pe.matmul(accA[i][e * HALF:(e + 1) * HALF, q * P:(q + 1) * P],
                                                     G[:, i, q * P + e * HALF:q * P + (e + 1) * HALF],
                                                     U[:, 2 * q + e, :], start=True, stop=True)
                        last.then_inc(T.sem, 1)
                        pe.wait_ge(*A.after("keven", r))
                        pe.wait_ge(in_t, r * (16 * STEP) + 16 * STEP)
                        pe.wait_ge(*R.after("z", r))
                        for q in range(QPAIRS):
                            for e in range(2):
                                rows = slice(e * HALF, (e + 1) * HALF)
                                o = q * P
                                pe.matmul(accB[e][:, o:o + P], Tz[:, 2 * q + e, :], U[:, 2 * q + e, :], start=True, stop=False)
                                for i in range(2):
                                    last = pe.matmul(accB[e][:, o + 1:o + P], ca[rows, i, q * NQ + GROUP_W:(q + 1) * NQ],
                                                     z[i][rows, o:o + P - 1], start=False, stop=(i == 1))
                        last.then_inc(T.sem, 1)

        with ExitStack() as es:
            hH = es.enter_context(nc.sbuf_tensor("s5_gH", [P, KD, S], F32R))
            hL = es.enter_context(nc.sbuf_tensor("s5_gL", [P, KD, S], F32R))
            sg = es.enter_context(nc.sbuf_tensor("s5_sig", [P, S], F32))
            with ExitStack() as g:
                yf = g.enter_context(nc.sbuf_tensor("s5_yf", [P, 2, S], F32))
                in_y = [sem(f"s5_y_landed{b}") for b in range(2)]
                A = Steps(sem("s5_gelu_act"), ["gelu", "hi"])
                V = Steps(sem("s5_gelu_dve"), ["skip", "lo"])
                with nc.Block() as block:
                    @block.sync
                    def _(sp):
                        for k in range(KD):
                            if k >= 2:
                                sp.wait_ge(*V.after("lo", k - 2))
                            sp.dma_start(yf[:, k % 2, :], y_d[k * P:(k + 1) * P].rearrange("p j c -> p (j c)")
                                         ).then_inc(in_y[k % 2], 16)

                    @block.vector
                    def _(dve):
                        for k in range(KD):
                            dve.wait_ge(in_y[k % 2], k // 2 * 16 + 16)
                            d0 = COLS["ssm_d_2"][0] + k
                            dve.scalar_tensor_tensor(out=yf[:, k % 2, :], in0=hf[:, k, :], scalar=col[:, d0:d0 + 1],
                                                     in1=yf[:, k % 2, :], op0=ALU.mult, op1=ALU.add).then_inc(V.sem, 1)
                            dve.wait_ge(*A.after("hi", k))
                            dve.tensor_tensor(hL[:, k, :].rearrange("p (c j) -> p c j", j=STEP), by_step(yf[:, k % 2, :]),
                                              hH[:, k, :].rearrange("p (c j) -> p c j", j=STEP).bitcast(F32),
                                              ALU.subtract).then_inc(V.sem, 1)

                    @block.scalar
                    def _(act):
                        for k in range(KD):
                            act.wait_ge(*V.after("skip", k))
                            act.activation(yf[:, k % 2, :], yf[:, k % 2, :], ACT.Gelu_apprx_tanh).then_inc(A.sem, 1)
                            act.wait_ge(*A.after("gelu", k))
                            act.activation(hH[:, k, :].rearrange("p (c j) -> p c j", j=STEP), by_step(yf[:, k % 2, :]),
                                           ACT.Copy).then_inc(A.sem, 1)

            s_sig = sem("s5_gate_sigmoid")
            s_used = sem("s5_sigmoid_used")
            s_val = sem("s5_value_gated")
            vg = es.enter_context(nc.sbuf_tensor("s5_vg", [P, S], F32))
            with nc.Block() as block:
                def gate_tile(act, i, done, acc, psum_free):
                    act.wait_ge(s_used, i + 1)
                    act.wait_ge(tile_done, done)
                    act.activation(sg[:, :], acc[:, :], ACT.Sigmoid).then_inc(s_sig, 1)
                    act.wait_ge(s_sig, i + 1)
                    act.sem_inc(psum_free, 1)

                def value_tile(dve, i, done, acc, psum_free):
                    dve.wait_ge(s_sig, i + 1)
                    dve.wait_ge(tile_done, done)
                    dve.tensor_tensor(vg[:, :], acc[:, :], sg[:, :], ALU.mult).then_inc(s_val, 1)
                    dve.wait_ge(s_val, i + 1)
                    dve.sem_inc(psum_free, 1)
                    dve.sem_inc(s_used, 1)
                    x_m = at(xT, i)
                    dve.scalar_tensor_tensor(out=x_m, in0=vg[:, :], scalar=mods[:, bass.ds(i + (layer * 48 + 2 * KD), 1)],
                                             in1=x_m, op0=ALU.mult, op1=ALU.add).then_inc(s_x, 1)
                    dve.wait_ge(s_x, i + 1)
                s_x = sem("s5_residual_added")

                @block.gpsimd
                def _(pool):
                    pool.sem_inc(s_used, 1)
                env["weight_stream"]([dict(w=a["ssm_w_out_2"], K=KD, iters=KD, act=[gate_tile, None], dve=[None, value_tile],
                                           rhs=lambda q, k: (hH, hL)[q][:, k, :], cols=S, ready=None)], block)


def conv_mixer(nc, a, env, layer):
    sem, col, mods = (env[k] for k in ("sem", "col", "mods"))
    tile_done = env["tile_done"]
    with ExitStack() as es:
        with ExitStack() as g:
            hH = g.enter_context(nc.sbuf_tensor("conv_hH", [P, KD, S], F32R))
            hL = g.enter_context(nc.sbuf_tensor("conv_hL", [P, KD, S], F32R))
            mH = g.enter_context(nc.sbuf_tensor("conv_mH", [P, KD, S], F32R))
            mL = g.enter_context(nc.sbuf_tensor("conv_mL", [P, KD, S], F32R))
            ct = g.enter_context(nc.sbuf_tensor("conv_c", [P, S], F32))
            cv = g.enter_context(nc.sbuf_tensor("conv_cv", [P, S], F32))
            w3 = g.enter_context(nc.sbuf_tensor("conv_taps", [P, 3], F32))
            s_c = sem("conv_c_copied")
            V = Steps(sem("conv_dve"), ["taps", "cv", "t2", "t1", "t0", "gated", "lo"])
            s_hi = sem("conv_hi")

            def c_tile(m_of):
                def epi(act, i, done, acc, psum_free):
                    m = m_of(i)
                    act.wait_ge(s_cfree, m + 1)
                    act.wait_ge(tile_done, done)
                    act.activation(ct[:, :], acc[:, :], ACT.Copy).then_inc(s_c, 1)
                    act.wait_ge(s_c, m + 1)
                    act.sem_inc(psum_free, 1)
                return epi
            s_cfree = sem("conv_c_free")
            cc = g.enter_context(nc.sbuf_tensor("conv_sum", [P, S], F32))
            before = env["modulated_norm"](2, layer, 0, bufs=[ct, cv, cc], hi=lambda k: hH[:, k, :], lo=lambda k: hL[:, k, :])

            def v_tile(m_of):
                def epi(dve, i, done, acc, psum_free):
                    m = m_of(i)
                    t0 = COLS["conv_w_2"][0]
                    dve.tensor_copy(w3[:, :], col[:, bass.ds(m * 3 + t0, 3)]).then_inc(V.sem, 1)
                    dve.wait_ge(s_c, m + 1)
                    dve.wait_ge(tile_done, done)
                    dve.tensor_tensor(cv[:, :], acc[:, :], ct[:, :], ALU.mult).then_inc(V.sem, 1)
                    dve.wait_ge(*V.after("cv", m))
                    dve.sem_inc(psum_free, 1)
                    dve.sem_inc(s_cfree, 1)
                    dve.tensor_scalar(cc[:, :], cv[:, :], w3[:, 2:3], None, ALU.mult).then_inc(V.sem, 1)
                    for n, back in (("t2", 1), ("t1", 2)):
                        dve.wait_ge(*V.after(n, m))
                        dve.scalar_tensor_tensor(out=cc[:, back:S], in0=cv[:, 0:S - back], scalar=w3[:, 2 - back:3 - back],
                                                 in1=cc[:, back:S], op0=ALU.mult, op1=ALU.add).then_inc(V.sem, 1)
                return epi

            def b_tile(m_of):
                def dve_epi(dve, i, done, acc, psum_free):
                    m = m_of(i)
                    dve.wait_ge(*V.after("t0", m))
                    dve.wait_ge(tile_done, done)
                    dve.tensor_tensor(cc[:, :], acc[:, :], cc[:, :], ALU.mult).then_inc(V.sem, 1)
                    dve.wait_ge(*V.after("gated", m))
                    dve.sem_inc(psum_free, 1)
                    dve.wait_ge(s_hi, m + 1)
                    dve.tensor_tensor(at(mL, m), cc[:, :], at(mH, m).bitcast(F32), ALU.subtract).then_inc(V.sem, 1)
                    dve.wait_ge(*V.after("lo", m))

                def act_epi(act, i, done, acc, psum_free):
                    m = m_of(i)
                    act.wait_ge(*V.after("gated", m))
                    act.activation(at(mH, m), cc[:, :], ACT.Copy).then_inc(s_hi, 1)
                return dve_epi, act_epi
            m0, m1 = (lambda i: i * 2), (lambda i: i * 2 + 1)
            g1 = layer * 48 + 2 * KD
            b0, b1 = b_tile(m0), b_tile(m1)
            with nc.Block() as block:
                @block.gpsimd
                def _(pool):
                    pool.sem_inc(s_cfree, 1)
                env["weight_stream"]([dict(w=a["conv_w_in_2"], K=KD, iters=KD // 2,
                                           act=[c_tile(m0), None, b0[1], c_tile(m1), None, b1[1]],
                                           dve=[None, v_tile(m0), b0[0], None, v_tile(m1), b1[0]],
                                           rhs=lambda q, k: (hH, hL)[q][:, k, :], cols=S, ready=None),
                                      dict(w=a["conv_w_out_2"], K=KD, iters=KD // 2, act=[None, None],
                                           dve=[env["add_to_x"](0, g1), env["add_to_x"](1, g1)],
                                           rhs=lambda q, k: (mH, mL)[q][:, k, :], cols=S,
                                           ready=V.after("lo", KD - 1))], block, before)


def swiglu(nc, a, env, layer):
    sem = env["sem"]
    tile_done = env["tile_done"]
    with ExitStack() as es:
        hH = es.enter_context(nc.sbuf_tensor(f"ffn_hH{layer}", [P, KD, S], F32R))
        hL = es.enter_context(nc.sbuf_tensor(f"ffn_hL{layer}", [P, KD, S], F32R))
        n = max(FFN_PARTS)
        gH = es.enter_context(nc.sbuf_tensor(f"ffn_gH{layer}", [P, n, S], F32R))
        gL = es.enter_context(nc.sbuf_tensor(f"ffn_gL{layer}", [P, n, S], F32R))
        sg = es.enter_context(nc.sbuf_tensor(f"ffn_silu{layer}", [P, S], F32))
        gb = es.enter_context(nc.sbuf_tensor(f"ffn_g{layer}", [P, S], F32))
        tot = es.enter_context(nc.sbuf_tensor(f"ffn_squares{layer}", [P, S], F32))
        before = env["modulated_norm"](2 * layer + 1, layer, 3, bufs=[sg, gb, tot],
                                       hi=lambda k: hH[:, k, :], lo=lambda k: hL[:, k, :])
        s_silu = sem(f"ffn_silu_done{layer}")
        s_g = sem(f"ffn_gated{layer}")
        s_hi = sem(f"ffn_hi{layer}")
        s_lo = sem(f"ffn_lo{layer}")

        def part(f0):
            def gate_act(act, i, done, acc, psum_free):
                act.wait_ge(s_g, i + (f0 + 1))
                act.wait_ge(tile_done, done)
                act.activation(sg[:, :], acc[:, :], ACT.Silu).then_inc(s_silu, 1)
                act.wait_ge(s_silu, i + (f0 + 1))
                act.sem_inc(psum_free, 1)

            def up_dve(dve, i, done, acc, psum_free):
                dve.wait_ge(s_silu, i + (f0 + 1))
                dve.wait_ge(tile_done, done)
                dve.tensor_tensor(gb[:, :], acc[:, :], sg[:, :], ALU.mult).then_inc(s_g, 1)
                dve.wait_ge(s_g, i + (f0 + 2))
                dve.sem_inc(psum_free, 1)
                dve.wait_ge(s_hi, i + (f0 + 1))
                dve.tensor_tensor(at(gL, i), gb[:, :], at(gH, i).bitcast(F32), ALU.subtract).then_inc(s_lo, 1)
                dve.wait_ge(s_lo, i + (f0 + 1))

            def up_act(act, i, done, acc, psum_free):
                act.wait_ge(s_g, i + (f0 + 2))
                act.activation(at(gH, i), gb[:, :], ACT.Copy).then_inc(s_hi, 1)
            return gate_act, up_dve, up_act
        segs = []
        f0 = 0
        g2 = layer * 48 + 5 * KD
        for k in FFN_PARTS:
            gate_act, up_dve, up_act = part(f0)
            segs.append(dict(w=a["w_ffn_in_2"][layer, 2 * f0:2 * (f0 + k)], K=KD, iters=k, act=[gate_act, up_act],
                             dve=[None, up_dve], rhs=lambda q, kk: (hH, hL)[q][:, kk, :], cols=S, ready=None))
            segs.append(dict(w=a[f"w_ffn_out_{k}_{f0}_2"][layer], K=k, iters=KD // 2, act=[None, None],
                             dve=[env["add_to_x"](0, g2), env["add_to_x"](1, g2)],
                             rhs=lambda q, kk: (gH, gL)[q][:, kk, :], cols=S, ready=(s_lo, f0 + k)))
            f0 += k
        with nc.Block() as block:
            @block.gpsimd
            def _(pool):
                pool.sem_inc(s_g, 1)
            env["weight_stream"](segs, block, before)


def kernel(**inputs):
    import numpy as np
    import concourse.bacc as _bacc
    from concourse.bass_utils import run_bass_kernel_spmd as _run

    def tiles(w):
        k,n=w.shape
        return np.ascontiguousarray(w.reshape(k//P,P,n//P,P).transpose(2,1,0,3).reshape(n//P,P,k))
    def cols(v):
        return v.reshape(-1,P).T
    def layout(z):
        I={}
        I['xT']=z['x'][0].T
        I['memT']=z['mem'][0].T
        H=4
        conv=np.stack([cols(z['conv_w'][0][t]) for t in range(4)]+[cols(z['conv_b'][0])],2)
        ms=np.stack([cols(z['mnorm_g'][0]),cols(z['skip_m'][0])],2)
        I['cols']=np.concatenate([cols(z['norm_g'][0]),cols(z['mem_norm_g'][0]),cols(z['final_g']),conv.reshape(P,-1),ms.reshape(P,-1),
          cols(z['dnorm_g'][0]),cols(z['norm1_g_2']),cols(z['norm2_g_2']),cols(z['b_ada_2']),cols(z['ssm_d_2'][0]),
          np.stack([cols(z['conv_w_2'][0][t]) for t in range(3)],2).reshape(P,-1),cols(z['final_g_2']),cols(z['c_2'][0])],1)
        I['ident']=np.eye(P,dtype=np.float32)
        I['later']=np.where(np.arange(P)[:,None]<=np.arange(P)[None,:],0,-1e30).astype(np.float32)
        I['future']=I['later'].T
        I['w_in']=tiles(z['w_in'][0])
        I['w_ada_2']=np.concatenate([tiles(z['w_ada_2'][l]) for l in range(2)])
        wo=z['w_out'][0].reshape(3,512,1024)
        I['w_out']=np.stack([tiles(wo[i]) for i in range(3)])
        I['w_qkv']=np.concatenate([z['wq_m'][0],z['wk_m'][0],z['wv_m'][0]],2)
        I['w_if']=z['w_if'][0].reshape(3,H,P,8).transpose(1,2,0,3).reshape(H,P,24)
        I['b_if']=z['b_if'][0].reshape(2,H).T
        I['lam']=np.stack([z['lam_q1'][0],z['lam_q2'][0],z['lam_k1'][0],z['lam_k2'][0]],1)
        I['w_mem_kv']=tiles(z['w_mem_kv'][0])
        I['step_no']=np.ascontiguousarray(np.broadcast_to(np.arange(128,dtype=np.float32),(P,128)))
        def state(v):
            return v.reshape(4,8,2,64).transpose(0,2,3,1).reshape(4,P,8)
        ls=np.broadcast_to(z['ssm_log_step_2'][0][:,None],(64,64))
        I['ssm_a']=np.stack([state(z['ssm_a_re_2'][0]),state(z['ssm_a_im_2'][0]),state(ls)],2)
        B=lambda v: v.reshape(4,8,2,64,16).transpose(0,2,3,1,4).reshape(4,P,128)
        C=lambda v: v.reshape(4,8,2,16,64).transpose(0,2,4,1,3).reshape(4,P,128)
        I['ssm_bc']=np.stack([B(z['ssm_b_re_2'][0]),B(z['ssm_b_im_2'][0]),C(z['ssm_c_re_2'][0]),C(z['ssm_c_im_2'][0])],2)
        def twos(w,order):
            n=w.shape[1]//len(order)
            t=[tiles(w[:,i*n:(i+1)*n]) for i in order]
            return np.stack(t,1).reshape(-1,P,w.shape[0])
        I['ssm_w_out_2']=twos(z['ssm_w_out_2'][0],(1,0))
        w=z['conv_w_in_2'][0]
        I['conv_w_in_2']=np.stack([tiles(w[:,i*1024:(i+1)*1024]) for i in (1,2,0)],1).reshape(-1,P,1024)
        I['conv_w_out_2']=tiles(z['conv_w_out_2'][0])
        I['w_ffn_in_2']=np.stack([twos(z['w_ffn_in_2'][l],(0,1)) for l in range(2)])
        f0=0
        for k in (8,8,6):
            I[f'w_ffn_out_{k}_{f0}_2']=np.stack([tiles(z['w_ffn_out_2'][l][f0*P:(f0+k)*P]) for l in range(2)]); f0+=k
        return {k:np.ascontiguousarray(v) for k,v in I.items()}

    laid = layout({k: np.asarray(v) for k, v in inputs.items()})
    nc = _bacc.Bacc("TRN2", target_bir_lowering=False, num_devices=1)
    arrays, args = {}, {}
    for name, v in laid.items():
        arrays[f"in_{name}"] = v
        args[name] = nc.dram_tensor(f"in_{name}", v.shape, mybir.dt.from_np(v.dtype), kind="ExternalInput").ap()
    out = nc.dram_tensor("out_xT", (D, S), F32, kind="ExternalOutput").ap()
    build(nc, args, out)
    r = _run(nc, [arrays], core_ids=[0])
    return np.ascontiguousarray(r.results[0]["out_xT"].T)[None]
```
